# Optimizing a Trainium2 kernel written in Bass

```python
import math
import jax, jax.numpy as jnp
from jax import lax
import numpy as np

D_MODEL = 2048
BATCH = 1
SEQ = 256
DEPTH = 2

HEAD_DIM = 128
A_HEADS = 8
A_DK = 128
A_DV = 128
A_CHUNK = 64
B_HEADS = 8
B_KV_GROUPS = 2
B_HPG = B_HEADS // B_KV_GROUPS
CMP_LEN = 32
CMP_STRIDE = 16
SLC_LEN = 64
N_SLC = 16
WIN = 512
B_QBLK = 64
C_HEADS = 8
MOBA_BLOCK = 256
MOBA_TOPK = 3
C_QBLK = 32
D_HEADS = 4
D_DK = 128
D_DV = 2 * D_DK
D_QBLK = 128
D_FF = ((8 * D_MODEL + 3 * 256 - 1) // (3 * 256)) * 256

DEEPNORM_ALPHA = (2 * DEPTH) ** 0.25
DEEPNORM_BETA = (8 * DEPTH) ** -0.25
N_EVEN = (DEPTH + 1) // 2
N_ODD = DEPTH // 2
NEG_INF = -1e30
FORCE_SCORE = 1e9
LN_EPS = 1e-5
RMS_EPS = 1e-6

AB_SPLITS = (A_HEADS * A_DK, A_HEADS * A_DK, A_HEADS * A_DV, A_HEADS * A_DV, B_HEADS * HEAD_DIM) + (B_KV_GROUPS * HEAD_DIM,) * 6 + (3 * B_HEADS,)
AB_IN = sum(AB_SPLITS)
AB_MIX = A_HEADS * A_DV + B_HEADS * HEAD_DIM
CD_SPLITS = (C_HEADS * HEAD_DIM,) * 3 + (D_HEADS * 2 * D_DK, D_HEADS * 2 * D_DK, D_HEADS * D_DV)
CD_IN = sum(CD_SPLITS)
CD_MIX = C_HEADS * HEAD_DIM + D_HEADS * D_DV

kernel_name = 'hybrid_hgrn2_nsa_moba_diffattn_deepnorm'

def _split(z, sizes):
    offs = np.cumsum(sizes)[:-1].tolist()
    return jnp.split(z, offs, axis=-1)

def _layer_norm(x, w, b):
    xf = x.astype(jnp.float32)
    mu = xf.mean(-1, keepdims=True)
    var = jnp.square(xf - mu).mean(-1, keepdims=True)
    return ((xf - mu) * lax.rsqrt(var + LN_EPS) * w.astype(jnp.float32) + b.astype(jnp.float32)).astype(x.dtype)

def _rms_norm(x, w):
    xf = x.astype(jnp.float32)
    return xf * lax.rsqrt(jnp.mean(xf * xf, -1, keepdims=True) + RMS_EPS) * w.astype(jnp.float32)

def _masked_softmax(s, mask):
    p = jax.nn.softmax(jnp.where(mask, s.astype(jnp.float32), NEG_INF), axis=-1)
    return p * mask

def _gather_blocks(blocks, idx):
    return jax.vmap(jax.vmap(lambda bl, ix: bl[ix]))(blocks, idx)

def _swiglu(h, w_in, w_out):
    g, u = jnp.split(h @ w_in, 2, axis=-1)
    return (jax.nn.silu(g) * u) @ w_out

def _hgrn2(q, f_raw, i, g, lb, norm_w):
    bsz, t_len, _ = q.shape
    dt = q.dtype
    nc = t_len // A_CHUNK
    f = lb + (1.0 - lb) * jax.nn.sigmoid(f_raw.astype(jnp.float32))
    logf = jnp.log(f)
    k = 1.0 - f
    qf = jax.nn.silu(q.astype(jnp.float32))

    def heads(z, d):
        return z.reshape(bsz, nc, A_CHUNK, A_HEADS, d).transpose(1, 0, 3, 2, 4)

    qc, kc, lc = heads(qf, A_DK), heads(k, A_DK), heads(logf, A_DK)
    vc = heads(i.astype(jnp.float32), A_DV)
    b = jnp.cumsum(lc, axis=3)
    b_last = b[..., -1:, :]
    q_t = qc * jnp.exp(b)
    k_t = kc * jnp.exp(-b)
    causal = jnp.tril(jnp.ones((A_CHUNK, A_CHUNK), dtype=bool))
    att = jnp.where(causal, jnp.einsum('nbhcd,nbhsd->nbhcs', q_t, k_t), 0.0)
    o_intra = jnp.einsum('nbhcs,nbhsv->nbhcv', att, vc)
    u = jnp.einsum('nbhcd,nbhcv->nbhdv', kc * jnp.exp(b_last - b), vc)
    decay = jnp.exp(b_last[..., 0, :])

    def step(state, inp):
        qt, dec, uu = inp
        o = jnp.einsum('bhcd,bhdv->bhcv', qt, state)
        return dec[..., None] * state + uu, o

    s0 = jnp.zeros((bsz, A_HEADS, A_DK, A_DV), jnp.float32)
    _, o_inter = lax.scan(step, s0, (q_t, decay, u))
    o = (o_intra + o_inter).transpose(1, 0, 3, 2, 4).reshape(bsz, t_len, A_HEADS, A_DV)
    gate = jax.nn.silu(g.astype(jnp.float32)).reshape(bsz, t_len, A_HEADS, A_DV)
    o = _rms_norm(o, norm_w) * gate
    return o.reshape(bsz, t_len, A_HEADS * A_DV).astype(dt)

def _cmp_to_slc(p, nb):
    ratio = SLC_LEN // CMP_STRIDE
    n_over = CMP_LEN // CMP_STRIDE
    ax = p.ndim - 1
    right = ratio * nb - p.shape[-1]
    pp = jnp.pad(p, [(0, 0)] * ax + [(n_over - 1, right)])
    terms = []
    for m in range(ratio):
        for n in range(n_over):
            st = m - n + n_over - 1
            terms.append(lax.slice_in_dim(pp, st, st + ratio * (nb - 1) + 1, stride=ratio, axis=ax))
    return sum(terms)

def _nsa(q, k_c, v_c, k_s, v_s, k_w, v_w, gate, pos_k, w1k, w2k, pos_v, w1v, w2v):
    bsz, t_len, _ = q.shape
    dt = q.dtype
    scale = HEAD_DIM ** -0.5
    qh = q.reshape(bsz, t_len, B_KV_GROUPS, B_HPG, HEAD_DIM).transpose(0, 2, 3, 1, 4)

    def kv(z):
        return z.reshape(bsz, t_len, B_KV_GROUPS, HEAD_DIM).transpose(0, 2, 1, 3)

    n_cmp = (t_len - CMP_LEN) // CMP_STRIDE + 1
    cidx = np.arange(n_cmp)[:, None] * CMP_STRIDE + np.arange(CMP_LEN)[None, :]

    def compress(z, pos, w1, w2):
        blk = kv(z)[:, :, cidx] + pos
        hid = jax.nn.silu(blk.reshape(bsz, B_KV_GROUPS, n_cmp, CMP_LEN * HEAD_DIM) @ w1)
        return hid @ w2

    k_cmp = compress(k_c, pos_k, w1k, w2k)
    v_cmp = compress(v_c, pos_v, w1v, w2v)
    cmp_end = jnp.arange(n_cmp) * CMP_STRIDE + (CMP_LEN - 1)
    nb = t_len // SLC_LEN
    n_sel = min(N_SLC, nb)
    k_slc = kv(k_s).reshape(bsz, B_KV_GROUPS, nb, SLC_LEN, HEAD_DIM)
    v_slc = kv(v_s).reshape(bsz, B_KV_GROUPS, nb, SLC_LEN, HEAD_DIM)
    wpad = ((0, 0), (0, 0), (WIN, 0), (0, 0))
    k_win = jnp.pad(kv(k_w), wpad)
    v_win = jnp.pad(kv(v_w), wpad)
    gates = jax.nn.sigmoid(gate.astype(jnp.float32)).reshape(bsz, t_len, B_KV_GROUPS, B_HPG, 3).transpose(0, 2, 3, 1, 4)

    nqb = t_len // B_QBLK
    q_blocks = qh.reshape(bsz, B_KV_GROUPS, B_HPG, nqb, B_QBLK, HEAD_DIM).transpose(3, 0, 1, 2, 4, 5)
    g_blocks = gates.reshape(bsz, B_KV_GROUPS, B_HPG, nqb, B_QBLK, 3).transpose(3, 0, 1, 2, 4, 5)
    starts = jnp.arange(nqb, dtype=jnp.int32) * B_QBLK
    jb = jnp.arange(nb)
    lpos = jnp.arange(SLC_LEN)

    def block(args):
        qb, gb, q0 = args
        t = q0 + jnp.arange(B_QBLK)
        s = jnp.einsum('bghqd,bgnd->bghqn', qb, k_cmp) * scale
        p_c = _masked_softmax(s, cmp_end[None, :] <= t[:, None])
        o_c = jnp.einsum('bghqn,bgnd->bghqd', p_c.astype(dt), v_cmp)
        p_slc = _cmp_to_slc(p_c.sum(axis=2), nb)
        cur = t // SLC_LEN
        valid = jb[None, :] <= cur[:, None]
        forced = (jb[None, :] == 0) | (jb[None, :] == cur[:, None]) | (jb[None, :] == cur[:, None] - 1)
        score = jnp.where(valid, jnp.where(forced, FORCE_SCORE, p_slc), NEG_INF)
        _, idx = lax.top_k(score, n_sel)
        ks = _gather_blocks(k_slc, idx)
        vs = _gather_blocks(v_slc, idx)
        s = jnp.einsum('bghqd,bgqnld->bghqnl', qb, ks) * scale
        kpos = idx[..., None] * SLC_LEN + lpos
        m_s = (kpos <= t[:, None, None])[:, :, None]
        s = s.reshape(s.shape[:4] + (n_sel * SLC_LEN,))
        m_s = m_s.reshape(m_s.shape[:4] + (n_sel * SLC_LEN,))
        p_s = _masked_softmax(s, m_s)
        o_s = jnp.einsum('bghqk,bgqkd->bghqd', p_s.astype(dt), vs.reshape(vs.shape[:3] + (n_sel * SLC_LEN, HEAD_DIM)))
        kw = lax.dynamic_slice_in_dim(k_win, q0, WIN + B_QBLK, axis=2)
        vw = lax.dynamic_slice_in_dim(v_win, q0, WIN + B_QBLK, axis=2)
        wpos = q0 - WIN + jnp.arange(WIN + B_QBLK)
        m_w = (wpos[None, :] <= t[:, None]) & (wpos[None, :] > t[:, None] - WIN) & (wpos[None, :] >= 0)
        s = jnp.einsum('bghqd,bgkd->bghqk', qb, kw) * scale
        p_w = _masked_softmax(s, m_w)
        o_w = jnp.einsum('bghqk,bgkd->bghqd', p_w.astype(dt), vw)
        return (gb[..., 0:1] * o_c + gb[..., 1:2] * o_s + gb[..., 2:3] * o_w).astype(dt)

    o = lax.map(block, (q_blocks, g_blocks, starts))
    return o.transpose(1, 0, 4, 2, 3, 5).reshape(bsz, t_len, B_HEADS * HEAD_DIM)

def _moba(q, k, v):
    bsz, t_len, _ = q.shape
    dt = q.dtype
    scale = HEAD_DIM ** -0.5
    nbm = -(-t_len // MOBA_BLOCK)
    t_pad = nbm * MOBA_BLOCK

    def heads(z):
        return z.reshape(bsz, t_len, C_HEADS, HEAD_DIM).transpose(0, 2, 1, 3)

    qh = heads(q)
    pad = ((0, 0), (0, 0), (0, t_pad - t_len), (0, 0))
    kp = jnp.pad(heads(k), pad)
    vp = jnp.pad(heads(v), pad)
    k_blk = kp.reshape(bsz, C_HEADS, nbm, MOBA_BLOCK, HEAD_DIM)
    v_blk = vp.reshape(bsz, C_HEADS, nbm, MOBA_BLOCK, HEAD_DIM)
    k_mean = k_blk.astype(jnp.float32).mean(axis=3).astype(dt)
    n_top = min(MOBA_TOPK, max(nbm - 1, 1))
    nqb = t_len // C_QBLK
    q_blocks = qh.reshape(bsz, C_HEADS, nqb, C_QBLK, HEAD_DIM).transpose(2, 0, 1, 3, 4)
    starts = jnp.arange(nqb, dtype=jnp.int32) * C_QBLK
    jb = jnp.arange(nbm)

    def block(args):
        qb, q0 = args
        t = q0 + jnp.arange(C_QBLK)
        cur = q0 // MOBA_BLOCK
        gate = jnp.einsum('bhqd,bhnd->bhqn', qb, k_mean).astype(jnp.float32)
        gate = jnp.where(jb < cur, gate, NEG_INF)
        _, idx = lax.top_k(gate, n_top)
        sel_ok = idx < cur
        ks = _gather_blocks(k_blk, idx)
        vs = _gather_blocks(v_blk, idx)
        s_sel = jnp.einsum('bhqd,bhqnld->bhqnl', qb, ks).reshape(bsz, C_HEADS, C_QBLK, n_top * MOBA_BLOCK)
        m_sel = jnp.broadcast_to(sel_ok[..., None], sel_ok.shape + (MOBA_BLOCK,)).reshape(s_sel.shape)
        k_own = lax.dynamic_slice_in_dim(kp, cur * MOBA_BLOCK, MOBA_BLOCK, axis=2)
        v_own = lax.dynamic_slice_in_dim(vp, cur * MOBA_BLOCK, MOBA_BLOCK, axis=2)
        s_own = jnp.einsum('bhqd,bhkd->bhqk', qb, k_own)
        opos = cur * MOBA_BLOCK + jnp.arange(MOBA_BLOCK)
        m_own = jnp.broadcast_to(opos[None, :] <= t[:, None], s_own.shape)
        s = jnp.concatenate([s_sel, s_own], axis=-1) * scale
        m = jnp.concatenate([m_sel, m_own], axis=-1)
        p = _masked_softmax(s, m).astype(dt)
        n_sel_keys = n_top * MOBA_BLOCK
        o = jnp.einsum('bhqk,bhqkd->bhqd', p[..., :n_sel_keys], vs.reshape(bsz, C_HEADS, C_QBLK, n_sel_keys, HEAD_DIM))
        return o + jnp.einsum('bhqk,bhkd->bhqd', p[..., n_sel_keys:], v_own)

    o = lax.map(block, (q_blocks, starts))
    return o.transpose(1, 0, 3, 2, 4).reshape(bsz, t_len, C_HEADS * HEAD_DIM)

def _diff_attn(q, k, v, lq1, lk1, lq2, lk2, subln_w, layer_idx):
    bsz, t_len, _ = q.shape
    dt = q.dtype
    scale = D_DK ** -0.5
    lam_init = 0.8 - 0.6 * math.exp(-0.3 * layer_idx)
    f32 = jnp.float32
    lam = (jnp.exp(jnp.sum(lq1.astype(f32) * lk1.astype(f32))) - jnp.exp(jnp.sum(lq2.astype(f32) * lk2.astype(f32))) + lam_init)
    qh = q.reshape(bsz, t_len, D_HEADS, 2, D_DK).transpose(0, 2, 3, 1, 4)
    kh = k.reshape(bsz, t_len, D_HEADS, 2, D_DK).transpose(0, 2, 3, 1, 4)
    vh = v.reshape(bsz, t_len, D_HEADS, D_DV).transpose(0, 2, 1, 3)
    nqb = t_len // D_QBLK
    q_blocks = qh.reshape(bsz, D_HEADS, 2, nqb, D_QBLK, D_DK).transpose(3, 0, 1, 2, 4, 5)
    starts = jnp.arange(nqb, dtype=jnp.int32) * D_QBLK
    kpos = jnp.arange(t_len)

    def block(args):
        qb, q0 = args
        t = q0 + jnp.arange(D_QBLK)
        s = jnp.einsum('bhmqd,bhmkd->bhmqk', qb, kh) * scale
        p = _masked_softmax(s, kpos[None, :] <= t[:, None])
        w = p[:, :, 0] - lam * p[:, :, 1]
        return jnp.einsum('bhqk,bhkv->bhqv', w.astype(dt), vh)

    o = lax.map(block, (q_blocks, starts))
    o = o.transpose(1, 0, 3, 2, 4).reshape(bsz, t_len, D_HEADS, D_DV)
    o = _rms_norm(o, subln_w) * (1.0 - lam_init)
    return o.reshape(bsz, t_len, D_HEADS * D_DV).astype(dt)

def setup_inputs(seed: int = 0) -> dict:
    key = jax.random.key(seed)
    ks = jax.random.split(key, 22)

    def nrm(k, shape, s):
        return jax.random.normal(k, shape, jnp.float32) * s

    return {
        'x': nrm(ks[0], (BATCH, SEQ, D_MODEL), 1.0),
        'ln_w': 1.0 + nrm(ks[1], (DEPTH, 2, D_MODEL), 0.05),
        'ln_b': nrm(ks[2], (DEPTH, 2, D_MODEL), 0.02),
        'ffn_w_in': nrm(ks[3], (DEPTH, D_MODEL, 2 * D_FF), D_MODEL ** -0.5),
        'ffn_w_out': nrm(ks[4], (DEPTH, D_FF, D_MODEL), DEEPNORM_BETA * D_FF ** -0.5),
        'ab_w_in': nrm(ks[5], (N_EVEN, D_MODEL, AB_IN), D_MODEL ** -0.5),
        'ab_w_out': nrm(ks[6], (N_EVEN, AB_MIX, D_MODEL), DEEPNORM_BETA * AB_MIX ** -0.5),
        'hgrn_lower_bounds': nrm(ks[7], (DEPTH + 1, A_HEADS * A_DK), 0.1),
        'hgrn_norm_w': 1.0 + nrm(ks[8], (N_EVEN, A_DV), 0.05),
        'nsa_cmp_pos_k': nrm(ks[9], (N_EVEN, CMP_LEN, HEAD_DIM), 0.02),
        'nsa_cmp_k_w1': nrm(ks[10], (N_EVEN, CMP_LEN * HEAD_DIM, HEAD_DIM), (CMP_LEN * HEAD_DIM) ** -0.5),
        'nsa_cmp_k_w2': nrm(ks[11], (N_EVEN, HEAD_DIM, HEAD_DIM), HEAD_DIM ** -0.5),
        'nsa_cmp_pos_v': nrm(ks[12], (N_EVEN, CMP_LEN, HEAD_DIM), 0.02),
        'nsa_cmp_v_w1': nrm(ks[13], (N_EVEN, CMP_LEN * HEAD_DIM, HEAD_DIM), (CMP_LEN * HEAD_DIM) ** -0.5),
        'nsa_cmp_v_w2': nrm(ks[14], (N_EVEN, HEAD_DIM, HEAD_DIM), HEAD_DIM ** -0.5),
        'cd_w_in': nrm(ks[15], (N_ODD, D_MODEL, CD_IN), D_MODEL ** -0.5),
        'cd_w_out': nrm(ks[16], (N_ODD, CD_MIX, D_MODEL), DEEPNORM_BETA * CD_MIX ** -0.5),
        'diff_lambda_q1': nrm(ks[17], (N_ODD, D_DK), 0.1),
        'diff_lambda_k1': nrm(ks[18], (N_ODD, D_DK), 0.1),
        'diff_lambda_q2': nrm(ks[19], (N_ODD, D_DK), 0.1),
        'diff_lambda_k2': nrm(ks[20], (N_ODD, D_DK), 0.1),
        'diff_subln_w': 1.0 + nrm(ks[21], (N_ODD, D_DV), 0.05),
    }

def reference(x, ln_w, ln_b, ffn_w_in, ffn_w_out, ab_w_in, ab_w_out, hgrn_lower_bounds, hgrn_norm_w,
              nsa_cmp_pos_k, nsa_cmp_k_w1, nsa_cmp_k_w2, nsa_cmp_pos_v, nsa_cmp_v_w1, nsa_cmp_v_w2,
              cd_w_in, cd_w_out, diff_lambda_q1, diff_lambda_k1, diff_lambda_q2, diff_lambda_k2, diff_subln_w):
    lb_all = jnp.cumsum(jax.nn.softmax(hgrn_lower_bounds.astype(jnp.float32), axis=0), axis=0)
    h = x
    for layer in range(DEPTH):
        if layer % 2 == 0:
            e = layer // 2
            (a_q, a_f, a_i, a_g, b_q, b_kc, b_vc, b_ks, b_vs, b_kw, b_vw, b_g) = _split(h @ ab_w_in[e], AB_SPLITS)
            o_a = _hgrn2(a_q, a_f, a_i, a_g, lb_all[layer], hgrn_norm_w[e])
            o_b = _nsa(b_q, b_kc, b_vc, b_ks, b_vs, b_kw, b_vw, b_g,
                       nsa_cmp_pos_k[e], nsa_cmp_k_w1[e], nsa_cmp_k_w2[e],
                       nsa_cmp_pos_v[e], nsa_cmp_v_w1[e], nsa_cmp_v_w2[e])
            mix = jnp.concatenate([o_a, o_b], axis=-1) @ ab_w_out[e]
        else:
            o_idx = layer // 2
            (c_q, c_k, c_v, d_q, d_k, d_v) = _split(h @ cd_w_in[o_idx], CD_SPLITS)
            o_c = _moba(c_q, c_k, c_v)
            o_d = _diff_attn(d_q, d_k, d_v, diff_lambda_q1[o_idx], diff_lambda_k1[o_idx],
                             diff_lambda_q2[o_idx], diff_lambda_k2[o_idx], diff_subln_w[o_idx], layer)
            mix = jnp.concatenate([o_c, o_d], axis=-1) @ cd_w_out[o_idx]
        h = _layer_norm(DEEPNORM_ALPHA * h + mix, ln_w[layer, 0], ln_b[layer, 0])
        h = _layer_norm(DEEPNORM_ALPHA * h + _swiglu(h, ffn_w_in[layer], ffn_w_out[layer]), ln_w[layer, 1], ln_b[layer, 1])
    return h


_drawn_inputs = setup_inputs


def setup_inputs(seed=0):
    import zlib

    import numpy as np

    out = dict(_drawn_inputs(seed))
    spreads = {}
    factors = {'hgrn_lower_bounds': 8.0,
     'hgrn_norm_w': 6.78,
     'nsa_cmp_pos_k': 36.512,
     'nsa_cmp_k_w1': 3.668,
     'nsa_cmp_k_w2': 3.89,
     'nsa_cmp_pos_v': 8.0,
     'diff_lambda_q1': 18.928,
     'diff_lambda_k1': 3.625,
     'diff_lambda_q2': 3.594,
     'diff_lambda_k2': 5.524,
     'diff_subln_w': 7.208}
    for name, (base, spread) in spreads.items():
        noise = np.random.default_rng([zlib.crc32(name.encode()), seed]).standard_normal(out[name].shape)
        drawn = base * np.exp(spread * noise) if base else spread * noise
        out[name] = __import__('jax').numpy.asarray(drawn.astype(out[name].dtype))
    for name, factor in factors.items():
        out[name] = (out[name] * factor).astype(out[name].dtype)
    return out
```

```python
import math
from contextlib import ExitStack

import concourse.bass as bass
from concourse import mybir

F32 = mybir.dt.float32
F32R = mybir.dt.float32r
BF16 = mybir.dt.bfloat16
U32 = mybir.dt.uint32
ACT = mybir.ActivationFunctionType
ALU = mybir.AluOpType
AX = mybir.AxisListType

P = 128
T = 256
NT = T // P
D = 2048
KT = D // P
FF = 5632
HD = 128
CK = 2
CW = 512
UC = KT // CK
RAW_RING = 4
SPLIT_RING = 4
LOAD = 16 * CK
LEAD = SPLIT_RING - 1
NB = D // CW
CMP_LEN, CMP_STRIDE = 32, 16
NCMP = (T - CMP_LEN) // CMP_STRIDE + 1
HPG = 4
HCHUNK = 64
NHC = T // HCHUNK
ALPHA = 4 ** 0.25
SCALE = HD ** -0.5
NEG = -1e30
LN_EPS, RMS_EPS = 1e-5, 1e-6
LAM_INIT = 0.8 - 0.6 * math.exp(-0.3)
LN_EXP_SET = 6
SILU_SET = 18
EXP_CAP = 1.5e19

FFN_STEPS = FF // (2 * T)
FFN_CHUNKS = 2 * UC + 2 * NB
OUT_ORDER = [(0, 0), (1, 0), (0, 1), (1, 1), (2, 0), (2, 1), (3, 0), (3, 1)]
FFN_BANKS = [(4, 5), (6, 7), (0, 1), (2, 3)]
FFN_ACC = NB * (FFN_STEPS + 1)

AB_NSA = 4096
AB_KC, AB_KS, AB_GATE = AB_NSA + 1024, AB_NSA + 1536, AB_NSA + 2560
NGATE = 24

OUT_STREAM = ([(0, j) for j in range(UC - 1)] + [(1, j) for j in range(4)] + [(0, UC - 1)]
              + [(1, j) for j in range(4, UC)] + [(cb, j) for cb in range(2, NB) for j in range(UC)])
OUT0_END = OUT_STREAM.index((0, UC - 1)) + 1 - UC
UNITS0 = ["cmp", "keys", "values", "q0", "q1"] + [f"h{h}" for h in range(8)] + ["out"] * NB
UNITS1 = ["mv0", "mp0", "mp1", "mv1", "mp2", "mp3", "dv0", "dp0", "dp1", "dv1", "dp2", "dp3"] + ["out"] * NB
WORK1 = {2: ("moba", 0), 3: ("moba", 1), 5: ("moba", 2), 6: ("moba", 3),
         8: ("diff", 0), 9: ("diff", 1), 11: ("diff", 2), 12: ("diff", 3)}
FFN0 = len(UNITS0) * UC
L1 = FFN0 + FFN_CHUNKS * FFN_STEPS
FFN1 = L1 + len(UNITS1) * UC
N_IN0 = len(UNITS0) - NB
N_MAPS0 = 16
N_PLAIN0 = 8
N_NORM0 = 8

C_LB, C_NORM, C_SUB, C_LAM, C_POS, C_END = 0, 24, 25, 27, 31, 95


def nsa_head(u):
    return u - 5 if 5 <= u < 13 else None


def hgrn_head(u):
    return u - 6 if 6 <= u < 14 else None


def out_ktile(layer, j):
    k = CK * j
    return (k + 8) % KT if layer == 0 else k


def acc_act_count(layer, u):
    return layer * N_IN0 + u + 1


def acc_dve_count(layer, u):
    return layer * len(UNITS0) + u + 1


def build(nc, x, ln_w, ln_b, ffn_w_in, ffn_w_out, ab_w_in, ab_w_out, hgrn_lower_bounds, hgrn_norm_w,
          nsa_cmp_pos_k, nsa_cmp_k_w1, nsa_cmp_k_w2, nsa_cmp_pos_v, nsa_cmp_v_w1, nsa_cmp_v_w2,
          cd_w_in, cd_w_out, diff_lambda_q1, diff_lambda_k1, diff_lambda_q2, diff_lambda_k2,
          diff_subln_w, out):
    with ExitStack() as ctx:
        def sb(name, shape, dt=F32):
            return ctx.enter_context(nc.sbuf_tensor(name, shape, dt))

        def sem(name):
            return ctx.enter_context(nc.semaphore(name))

        res = sb("res", [P, NT, D])
        wb = sb("wb", [P, 2, D])
        w1 = wb[:].rearrange("p a (l j) -> p (a l) j", j=HD)
        xh = sb("xh", [P, KT, T], F32R)
        xl = sb("xl", [P, KT, T], F32R)
        oh = sb("oh", [P, KT, T], F32R)
        ol = sb("ol", [P, KT, T], F32R)
        fh, fl = oh[:, 0:4, :], ol[:, 0:4, :]
        raw = [sb(f"raw{i}", [P, CK, CW]) for i in range(RAW_RING)]
        wh = [sb(f"wh{i}", [P, CK, CW], F32R) for i in range(SPLIT_RING)]
        wl = [sb(f"wl{i}", [P, CK, CW], F32R) for i in range(SPLIT_RING)]
        scratch = sb("scratch", [P, 3, CK * T])
        xfull = [scratch[:, i, :].rearrange("p (k t) -> p k t", k=CK) for i in range(3)]
        blk = scratch[:].rearrange("p a b -> p (a b)")[:, 0:CMP_LEN * 2 * NCMP].rearrange(
            "p (l g n) -> p l g n", l=CMP_LEN, g=2)
        ident = sb("ident", [P, P])
        identb = sb("identb", [P, P], BF16)
        negmask = sb("negmask", [P, P], BF16)
        means = sb("means", [P, P])
        rows1 = sb("rows1", [P, P])
        rows2 = sb("rows2", [P, P])
        cols1 = sb("cols1", [P, P])
        cols2 = sb("cols2", [P, P])
        stats = sb("stats", [P, NT, NB, 6])
        mv = sb("mv", [P, NT, 2])
        lnvar = sb("lnvar", [P, NT])
        rstd = sb("rstd", [P, NT])
        shift = sb("shift", [P, 1])
        eps_ln = sb("eps_ln", [P, 1])
        eps_rms = sb("eps_rms", [P, 1])
        one = sb("one", [P, 1])
        kT = sb("kT", [P, 4, T])
        vnat = sb("vnat", [P, NT, CW])
        qT = sb("qT", [P, 8, T])
        mx = sb("mx", [P, 2])
        negmx = sb("negmx", [P, 2])
        rowsum = sb("rowsum", [P, 2, 2])
        fac = sb("fac", [P, 2, 2])
        prob = [sb(f"prob{i}", [P, 3 * P]) for i in range(2)]
        pT = sb("pT", [P, 3 * P])
        of = sb("of", [P, 2, T])
        sq = sb("sq", [P, 2, T])
        rootb = sq
        lam = sb("lam", [P, 8])
        cT = sb("cT", [P, 4, T])
        fs = cT[:, 0:2, :]
        ff = cT[:, 2:4, :]
        gw = sq[:].rearrange("p a t -> p (a t)")[:, 0:KT * NGATE].rearrange("p (k n) -> p k n", k=KT)
        gwh = sb("gwh", [P, KT, NGATE], F32R)
        gwl = sb("gwl", [P, KT, NGATE], F32R)
        gateT = of[0:NGATE, 0, :]
        gates = sb("gates", [P, NT, NGATE])
        hid = sb("hid", [P, 2 * NCMP])
        w2 = sb("w2", [P, 2, HD])
        kcmp = sb("kcmp", [P, 2 * NCMP])
        vcmp = sb("vcmp", [NCMP, 2, HD])
        cmask = sb("cmask", [P, NT * HPG, NCMP])
        cneg = sb("cneg", [P, NT * HPG, NCMP])
        pc = [sb(f"pc{g}", [P, NT * HPG, NCMP]) for g in range(2)]
        cmx = sb("cmx", [P, NT * HPG])
        csum = sb("csum", [P, NT * HPG])
        pcT = sb("pcT", [NCMP, T])
        lbc = sb("lbc", [P, 2, 8])
        lbt = sb("lbt", [P, 3, 8])
        lbm = sb("lbm", [P, 2, 8])
        omask = sb("omask", [P, NT, P], U32)
        reset = sb("reset", [P, T])
        hx = sb("hx", [P, 3, T])
        hv = sb("hv", [P, NT, HD])
        hg = sb("hg", [P, T])
        hk = sb("hk", [P, T])
        hb = sb("hb", [P, T])
        hs = sb("hs", [P, T])
        he = sb("he", [P, T])
        hn = sb("hn", [P, 2, T])
        hdec = sb("hdec", [P, NHC])
        hatt = sb("hatt", [P, NT, P])
        hk2 = sb("hk2", [P, NT, HD])
        hstate = sb("hstate", [P, NHC - 1, HD])

        bank = [ctx.enter_context(nc.psum_tensor(f"bank{i}", [P, CW], F32)) for i in range(8)]
        scores_ps, pT_ps, o_ps, misc_ps = bank[4], bank[5], bank[6], bank[7]

        def pair(ap):
            return ap[:].rearrange("p (a t) -> p a t", a=2)

        def acc_banks(u):
            return (bank[0], bank[1]) if u % 2 == 0 else (bank[2], bank[3])

        def row_cols(i):
            return pT_ps[:, i * P:(i + 1) * P]

        loaded = [sem(f"loaded{i}") for i in range(RAW_RING)]
        hi_done = sem("hi_done")
        lo_done = sem("lo_done")
        chunk_used = sem("chunk_used")
        acc_act = sem("acc_act")
        acc_dve = sem("acc_dve")
        x_loaded = [sem(f"x_loaded{q}") for q in range(NB)]
        rows_loaded = sem("rows_loaded")
        small_loaded = sem("small_loaded")
        w1_loaded = sem("w1_loaded")
        lnw_loaded = sem("lnw_loaded")
        const_ready = sem("const_ready")
        rows_turned = sem("rows_turned")
        cols_ready = sem("cols_ready")
        x_normed = sem("x_normed")
        x_normed_act = sem("x_normed_act")
        shift_ready = sem("shift_ready")
        x_turned = sem("x_turned")
        x_full = sem("x_full")
        x_hi = sem("x_hi")
        x_lo = sem("x_lo")
        var_ready = sem("var_ready")
        lnvar_ready = sem("lnvar_ready")
        rstd_ready = sem("rstd_ready")
        res_ready = sem("res_ready")
        pool_step = sem("pool_step")
        dve_step = sem("dve_step")
        act_step = sem("act_step")
        ffn_silu = sem("ffn_silu")
        ffn_h = sem("ffn_h")
        ffn_hh = sem("ffn_hh")
        ffn_hl = sem("ffn_hl")
        ffn_acc = sem("ffn_acc")
        s_scores = sem("s_scores")
        s_negmx = sem("s_negmx")
        s_exp = sem("s_exp")
        s_prob = sem("s_prob")
        s_pT = sem("s_pT")
        s_pTc = sem("s_pTc")
        s_pv = sem("s_pv")
        s_oh = sem("s_oh")
        s_ol = sem("s_ol")
        s_of = sem("s_of")
        s_sq = sem("s_sq")
        s_ms = sem("s_ms")
        s_root = sem("s_root")
        s_fin = sem("s_fin")
        s_foh = sem("s_foh")
        s_fol = sem("s_fol")
        s_lb = sem("s_lb")
        s_lbe = sem("s_lbe")
        s_lam = sem("s_lam")
        s_lam_ps = sem("s_lam_ps")
        s_lam_e = sem("s_lam_e")
        s_gwh = sem("s_gwh")
        s_gwl = sem("s_gwl")
        s_gate_ps = sem("s_gate_ps")
        s_gate_c = sem("s_gate_c")
        s_gate_T = sem("s_gate_T")
        s_gate_e = sem("s_gate_e")
        s_gates = sem("s_gates")
        s_blk = sem("s_blk")
        s_hid_ps = sem("s_hid_ps")
        s_hid_e = sem("s_hid_e")
        s_hid = sem("s_hid")
        s_cmp_ps = sem("s_cmp_ps")
        s_cmp = sem("s_cmp")
        s_cs = sem("s_cs")
        s_cz = sem("s_cz")
        s_ce = sem("s_ce")
        s_pc = sem("s_pc")
        s_pcT = sem("s_pcT")
        s_pcTc = sem("s_pcTc")
        s_he = sem("s_he")
        s_hcap = sem("s_hcap")
        s_hsig = sem("s_hsig")
        s_hf = sem("s_hf")
        s_hlog = sem("s_hlog")
        s_hsum = sem("s_hsum")
        s_hexp = sem("s_hexp")
        s_hqk = sem("s_hqk")
        s_hvT = sem("s_hvT")
        s_hv = sem("s_hv")
        s_hA = sem("s_hA")
        s_hatt = sem("s_hatt")
        s_hk2 = sem("s_hk2")
        s_hu = sem("s_hu")
        s_hu_even = sem("s_hu_even")
        s_hstate = sem("s_hstate")
        s_ho = sem("s_ho")
        out_ready = sem("out_ready")
        out_stored = sem("out_stored")

        w_ab = ab_w_in[0]
        ab_all = w_ab.rearrange("(k p) n -> p k n", p=P)
        ab_h = w_ab[:, 0:AB_NSA].rearrange("(k p) (s h c) -> p k s h c", p=P, s=4, h=8)
        ab_kv = w_ab[:, AB_KS:AB_GATE].rearrange("(k p) (a b c) -> p k a b c", p=P, a=2, b=2)
        cd_all = cd_w_in[0].rearrange("(k p) n -> p k n", p=P)
        cd_part = cd_w_in[0].rearrange("(k p) (m a c) -> p k m a c", p=P, m=2, a=3)
        w_out = [w[0].rearrange("(k p) n -> p k n", p=P) for w in (ab_w_out, cd_w_out)]
        ffn_in = [ffn_w_in[l].rearrange("(k p) (a n) -> p k a n", p=P, a=2) for l in range(2)]
        ffn_out = [ffn_w_out[l].rearrange("(k p) n -> p k n", p=P) for l in range(2)]
        x_view = x[0].rearrange("(t p) d -> p t d", p=P)
        out_view = out[0].rearrange("(t p) d -> p t d", p=P)
        w1_src = [w[0].rearrange("(l d) j -> d l j", d=HD) for w in (nsa_cmp_k_w1, nsa_cmp_v_w1)]

        block = ctx.enter_context(nc.Block())

        @block.sync
        def _(sp):
            def load(c, slot, src, parts=1):
                if not (isinstance(c, int) and c < RAW_RING):
                    sp.wait_ge(lo_done, c - RAW_RING + 1)
                for k in range(CK):
                    dst = raw[slot][:, k, :]
                    if parts > 1:
                        dst = dst.rearrange("p (a c) -> p a c", a=parts)
                    sp.dma_start(dst, src[:, k]).then_inc(loaded[slot], 16)

            def unit_chunk(layer, kind, cb, j):
                k = slice(CK * j, CK * j + CK)
                if kind == "out":
                    ko = out_ktile(layer, j)
                    return w_out[layer][:, ko:ko + CK, cb * CW:(cb + 1) * CW], 1
                if kind == "cmp":
                    return ab_all[:, k, AB_KC:AB_KC + CW], 1
                if kind == "keys":
                    return ab_kv[:, k, :, 0, :], 2
                if kind == "values":
                    return ab_kv[:, k, :, 1, :], 2
                i = int(kind[-1])
                if kind[0] == "q":
                    return ab_all[:, k, AB_NSA + CW * i:AB_NSA + CW * (i + 1)], 1
                if kind[0] == "h":
                    return ab_h[:, k, :, i, :], 4
                m = "md".index(kind[0])
                if kind[1] == "v":
                    return cd_part[:, k, m, 2, CW * i:CW * (i + 1)], 1
                return cd_part[:, k, m, 0:2, 2 * HD * i:2 * HD * (i + 1)], 2

            def mixers(layer, units, c0):
                for u, kind in enumerate(units):
                    for k in range(UC):
                        c = c0 + u * UC + k
                        cb, j = OUT_STREAM[(u - len(units) + NB) * UC + k] if kind == "out" else (None, k)
                        if c >= RAW_RING:
                            load(c, c % RAW_RING, *unit_chunk(layer, kind, cb, j))

            def ffn(layer, c0):
                with sp.Fori(0, FFN_STEPS) as i:
                    for half in range(2):
                        for j in range(UC):
                            n = half * UC + j
                            load(i * FFN_CHUNKS + (c0 + n), (c0 + n) % RAW_RING,
                                 ffn_in[layer][:, CK * j:CK * j + CK, :, bass.ds(i * (2 * T) + half * T, T)], 2)
                    for o, (cb, kk) in enumerate(OUT_ORDER):
                        n = 2 * UC + o
                        load(i * FFN_CHUNKS + (c0 + n), (c0 + n) % RAW_RING,
                             ffn_out[layer][:, bass.ds(i * 4 + CK * kk, CK), cb * CW:(cb + 1) * CW])

            for q in range(NB):
                cols = slice(q * CW, (q + 1) * CW)
                sp.dma_start(res[:, :, cols], x_view[:, :, cols]).then_inc(x_loaded[q], 16)
                load(q, q, *unit_chunk(0, UNITS0[0], None, q))
            for i, src in enumerate((ln_w, ln_b)):
                sp.dma_start(rows1[64 * i:64 * i + 64, :], src.rearrange("a b (k c) -> (a b k) c", c=P)).then_inc(rows_loaded, 16)
            sp.wait_ge(const_ready, 2)
            sp.dma_start(rows2[0:24, :], hgrn_lower_bounds.rearrange("a (k c) -> (a k) c", c=P)).then_inc(rows_loaded, 16)
            sp.dma_start(rows2[C_NORM:C_NORM + 1, :], hgrn_norm_w).then_inc(rows_loaded, 16)
            sp.dma_start(rows2[C_SUB:C_SUB + 2, :], diff_subln_w.rearrange("a (k c) -> (a k) c", c=P)).then_inc(rows_loaded, 16)
            for i, src in enumerate((diff_lambda_q1, diff_lambda_k1, diff_lambda_q2, diff_lambda_k2)):
                sp.dma_start(rows2[C_LAM + i:C_LAM + i + 1, :], src).then_inc(rows_loaded, 16)
            for i, src in enumerate((nsa_cmp_pos_k, nsa_cmp_pos_v)):
                at = C_POS + CMP_LEN * i
                sp.dma_start(rows2[at:at + CMP_LEN, :], src[0]).then_inc(rows_loaded, 16)
            sp.dma_start(gw, ab_all[:, :, AB_GATE:AB_GATE + NGATE]).then_inc(small_loaded, 16)
            sp.dma_start(w2[:, 0, :], nsa_cmp_k_w2[0]).then_inc(small_loaded, 16)
            sp.dma_start(w2[:, 1, :], nsa_cmp_v_w2[0]).then_inc(small_loaded, 16)
            mixers(0, UNITS0, 0)
            ffn(0, FFN0)
            mixers(1, UNITS1, L1)
            ffn(1, FFN1)
            for q in range(NB):
                sp.wait_ge(out_ready, q + 1)
                sp.dma_start(out_view[:, :, q * CW:(q + 1) * CW], res[:, :, q * CW:(q + 1) * CW]).then_inc(out_stored, 16)
            sp.wait_ge(out_stored, 16 * NB)

        @block.gpsimd
        def _(pool):
            steps = [0]

            def step(ins):
                steps[0] += 1
                ins.then_inc(pool_step, 1)
                pool.wait_ge(pool_step, steps[0])

            step(pool.memset(ident[:], 0.0))
            step(pool.affine_select(out=ident[:], in_=ident[:], compare_op=ALU.not_equal, fill=1.0, base=0,
                                    pattern=[[-1, P]], channel_multiplier=1))
            pool.tensor_copy(identb[:], ident[:]).then_inc(const_ready, 1)
            pool.memset(rows2[:], 0.0).then_inc(const_ready, 1)
            pool.memset(means[:], 1.0 / HD).then_inc(const_ready, 1)
            pool.memset(eps_ln[:], LN_EPS).then_inc(const_ready, 1)
            pool.memset(eps_rms[:], RMS_EPS).then_inc(const_ready, 1)
            pool.memset(one[:], 1.0).then_inc(const_ready, 1)
            step(pool.memset(negmask[:], 0.0))
            pool.affine_select(out=negmask[:], in_=negmask[:], compare_op=ALU.is_ge, fill=NEG, base=0,
                               pattern=[[-1, P]], channel_multiplier=1).then_inc(const_ready, 1)
            step(pool.memset(cmask[:], 1.0))
            for t in range(NT):
                part = cmask[:, t * HPG:(t + 1) * HPG, :]
                step(pool.affine_select(out=part, in_=part, compare_op=ALU.is_ge, fill=0.0,
                                        base=t * P - (CMP_LEN - 1), pattern=[[0, HPG], [-CMP_STRIDE, NCMP]],
                                        channel_multiplier=1))
            pool.tensor_scalar(cneg[:], cmask[:], -NEG, NEG, ALU.mult, ALU.add).then_inc(const_ready, 1)
            step(pool.memset(hatt[:], 1.0))
            step(pool.affine_select(out=hatt[:], in_=hatt[:], compare_op=ALU.is_ge, fill=0.0, base=0,
                                    pattern=[[0, NT], [1, P]], channel_multiplier=-1))
            second = hatt[:, :, HCHUNK:P]
            step(pool.affine_select(out=second, in_=second, compare_op=ALU.is_ge, fill=0.0, base=-HCHUNK,
                                    pattern=[[0, NT], [0, HCHUNK]], channel_multiplier=1))
            step(pool.tensor_copy(omask[:], hatt[:]))
            pool.memset(hatt[:], 0.0).then_inc(const_ready, 1)
            step(pool.memset(reset[:], 1.0))
            pool.memset(reset[:].rearrange("p (n c) -> p n c", c=HCHUNK)[:, :, 0:1], 0.0).then_inc(const_ready, 1)

            pool.wait_ge(x_turned, UC)
            pool.tensor_scalar(res[:], res[:], ALPHA, None, ALU.mult).then_inc(res_ready, 1)

            for h in range(8):
                pool.wait_ge(s_he, h + 1)
                pool.tensor_scalar(hx[:], hx[:], EXP_CAP, None, ALU.min).then_inc(s_hcap, 1)

            for n in range(4):
                if n == 0:
                    pool.wait_ge(s_hid_ps, 2)
                for a, src in enumerate((ln_w, ln_b)):
                    pool.dma_start(wb[:, a, :], src[n // 2, n % 2:n % 2 + 1, :].to_broadcast([P, D])).then_inc(lnw_loaded, 16)
                if n == 3:
                    break
                pool.wait_ge(lnw_loaded, 32 * (n + 1))
                step(pool.tensor_scalar(wb[:], wb[:], ALPHA, None, ALU.mult))
                pool.wait_ge(x_turned, UC * (n + 2))
                for t in range(NT):
                    step(pool.tensor_tensor(res[:, t, :], res[:, t, :], wb[:, 0, :], ALU.mult))
                    ins = pool.tensor_tensor(res[:, t, :], res[:, t, :], wb[:, 1, :], ALU.add)
                    if t < NT - 1:
                        step(ins)
                ins.then_inc(res_ready, 1)
                pool.wait_ge(res_ready, n + 2)

        @block.scalar
        def _(act):
            steps = [0]

            def load_ln_exp():
                nc.scalar.add_instruction(mybir.InstLoadActFuncSet(
                    name=nc.get_next_instruction_name(), act_func_set_id=LN_EXP_SET, ins=[], outs=[]))

            def step(ins):
                steps[0] += 1
                ins.then_inc(act_step, 1)
                act.wait_ge(act_step, steps[0])

            def load_silu():
                nc.scalar.add_instruction(mybir.InstLoadActFuncSet(
                    name=nc.get_next_instruction_name(), act_func_set_id=SILU_SET, ins=[], outs=[]))

            def split(c):
                act.wait_ge(loaded[c % RAW_RING], LOAD * (c // RAW_RING + 1))
                if c >= SPLIT_RING:
                    act.wait_ge(chunk_used, c - SPLIT_RING + 1)
                nc.scalar.activation(wh[c % SPLIT_RING][:], raw[c % RAW_RING][:], ACT.Copy).then_inc(hi_done, 1)

            def split_in_step(c, i):
                act.wait_ge(loaded[c % RAW_RING], i * (LOAD * FFN_CHUNKS // RAW_RING) + LOAD * (c // RAW_RING + 1))
                act.wait_ge(chunk_used, i * FFN_CHUNKS + (c - SPLIT_RING + 1))
                nc.scalar.activation(wh[c % SPLIT_RING][:], raw[c % RAW_RING][:], ACT.Copy).then_inc(hi_done, 1)

            def turned_hi(e, b):
                act.wait_ge(x_full, UC * e + b + 1)
                nc.scalar.activation(xh[:, CK * b:CK * b + CK, :], xfull[b % 3], ACT.Copy).then_inc(x_hi, 1)

            def layer_norm(n):
                act.wait_ge(var_ready, n + 1)
                nc.scalar.activation(lnvar[:], mv[:, :, 1], ACT.Ln, bias=eps_ln[:]).then_inc(lnvar_ready, 1)
                act.wait_ge(lnvar_ready, n + 1)
                nc.scalar.activation(rstd[:], lnvar[:], ACT.Exp, scale=-0.5).then_inc(rstd_ready, 1)
                act.wait_ge(rstd_ready, n + 1)
                act.wait_ge(shift_ready, n + 1)
                for q in range(NB):
                    part = res[:, 1, q * CW:(q + 1) * CW]
                    nc.scalar.activation(part, part, ACT.Identity, scale=rstd[:, 1:2], bias=shift[:]).then_inc(x_normed_act, 1)

            def soft_exp(m):
                act.wait_ge(s_negmx, m + 1)
                if m >= 2:
                    act.wait_ge(s_pT, m - 1 if m < 24 else 24 + (m - 24) // 2)
                for q, cols in enumerate((slice(0, P), slice(P, 3 * P))):
                    ins = nc.scalar.activation(prob[m % 2][:, cols], scores_ps[:, cols], ACT.Exp, bias=negmx[:, q:q + 1],
                                               scale=SCALE, accum_out=rowsum[:, m % 2, q:q + 1])
                ins.then_inc(s_exp, 1)

            def copy_pT(n):
                act.wait_ge(s_pT, n + 1)
                if n:
                    act.wait_ge(s_pv, n)
                nc.scalar.activation(pT[:], pT_ps[:, 0:3 * P], ACT.Copy).then_inc(s_pTc, 1)

            def plain_hi(kt, pv_count):
                act.wait_ge(s_pv, pv_count)
                nc.scalar.activation(oh[:, kt, :], o_ps[:, 0:T], ACT.Copy).then_inc(s_oh, 1)

            def norm_root(r, scale):
                act.wait_ge(s_ms, r + 1)
                step(nc.scalar.activation(rootb[:, 0, :], misc_ps[:, 0:T], ACT.Ln, scale=scale, bias=eps_rms[:]))
                nc.scalar.activation(rootb[:, 1, :], rootb[:, 0, :], ACT.Exp, scale=-0.5).then_inc(s_root, 1)

            def norm_hi(r, kt, w):
                act.wait_ge(s_fin, r + 1)
                nc.scalar.activation(oh[:, kt:kt + w, :], of[:, 0:w, :], ACT.Copy).then_inc(s_foh, 1)

            def read_acc(kind, u):
                A, B = acc_banks(u)
                if kind == "cmp":
                    return nc.scalar.activation(cT[:, 0:2, :], pair(A), ACT.Copy)
                if kind in ("values", "mv0", "mv1", "dv0", "dv1"):
                    return nc.scalar.activation(vnat[:, 0, :], A[:], ACT.Copy)
                if kind == "keys" or kind[1] == "p":
                    return nc.scalar.activation(kT[:, 0:2, :], pair(A), ACT.Copy)
                i = int(kind[1])
                if kind[0] == "q":
                    return nc.scalar.activation(qT[:, HPG * i:HPG * i + 2, :], pair(A), ACT.Copy)
                if i:
                    act.wait_ge(s_hf, 2 * i)
                nc.scalar.activation(hx[:, 0:2, :], pair(A), ACT.Exp, scale=-1.0)
                nc.scalar.activation(hx[:, 2, :], B[:, T:2 * T], ACT.Exp, scale=-1.0).then_inc(s_he, 1)
                return nc.scalar.activation(hv[:], B[:, 0:T].rearrange("p (t v) -> p t v", t=NT), ACT.Copy)

            def nsa(h, k):
                if k == 1:
                    soft_exp(2 * h)
                if k == 2:
                    act.wait_ge(s_pcT, h + 1)
                    nc.scalar.activation(pcT[:], pT_ps[0:NCMP, 0:T], ACT.Copy).then_inc(s_pcTc, 1)
                if k == 3:
                    copy_pT(2 * h)
                    soft_exp(2 * h + 1)
                if k == 5:
                    copy_pT(2 * h + 1)
                if k == 6:
                    plain_hi(8 + h, 2 * h + 2)

            def hgrn(h, k):
                if k == 1:
                    act.wait_ge(s_hcap, h + 1)
                    step(nc.scalar.activation(hx[:], hx[:], ACT.Ln, bias=one[:]))
                    nc.scalar.activation(hx[:], hx[:], ACT.Exp, scale=-1.0).then_inc(s_hsig, 1)
                if k == 2:
                    act.wait_ge(s_hf, 2 * h + 1)
                    nc.scalar.activation(hb[:], hx[:, 1, :], ACT.Ln).then_inc(s_hlog, 1)
                if k == 3:
                    act.wait_ge(s_hsum, h + 1)
                    nc.scalar.activation(he[:], hs[:], ACT.Exp)
                    nc.scalar.activation(hn[:, 0, :], hs[:], ACT.Exp, scale=-1.0)
                    for n in range(NHC):
                        s = slice(n * HCHUNK, (n + 1) * HCHUNK)
                        ins = nc.scalar.activation(hn[:, 1, s], hs[:, s], ACT.Exp, scale=-1.0,
                                                   bias=hs[:, (n + 1) * HCHUNK - 1:(n + 1) * HCHUNK])
                    ins.then_inc(s_hexp, 1)
                if k == 5:
                    act.wait_ge(s_hatt, h + 1)
                    nc.scalar.activation(hk2[:], misc_ps[:, T:2 * T].rearrange("p (t v) -> p t v", t=NT),
                                         ACT.Copy).then_inc(s_hk2, 1)
                if k == 7:
                    act.wait_ge(s_ho, h + 1)
                    if h:
                        act.wait_ge(s_fol, h)
                    nc.scalar.activation(of[:, 0, :], misc_ps[:, 0:T], ACT.Copy).then_inc(s_of, 1)
                if k == 8:
                    norm_root(h, 1.0)
                    norm_hi(h, h, 1)

            def moba(i, k):
                m = N_MAPS0 + 2 * i
                if k == 1:
                    soft_exp(m)
                if k == 2:
                    soft_exp(m + 1)
                if k == 3:
                    copy_pT(m)
                if k == 4:
                    plain_hi(2 * i, m + 1)
                if k == 5:
                    copy_pT(m + 1)
                if k == 6:
                    plain_hi(2 * i + 1, m + 2)

            def diff(d, k):
                m, n, r = 24 + 2 * d, 24 + d, N_NORM0 + d
                if k == 1:
                    soft_exp(m)
                if k == 2:
                    soft_exp(m + 1)
                if k == 4:
                    copy_pT(n)
                if k == 5:
                    act.wait_ge(s_pv, n + 1)
                    act.wait_ge(s_fol, r)
                    nc.scalar.activation(of[:], pair(o_ps), ACT.Copy).then_inc(s_of, 1)
                if k == 6:
                    norm_root(r, 0.5)
                    norm_hi(r, 8 + 2 * d, 2)

            def ffn_half(half, used, count):
                g = bank[2 * half]
                act.wait_ge(chunk_used, used)
                nc.scalar.activation(fs, pair(g), ACT.Silu).then_inc(ffn_silu, 1)
                act.wait_ge(ffn_h, count)
                nc.scalar.activation(fh[:, 2 * half:2 * half + 2, :], ff, ACT.Copy).then_inc(ffn_hh, 1)

            def ffn_step(layer, c0, i, last=False):
                for n in range(FFN_CHUNKS):
                    if n in (UC, 2 * UC):
                        half = n // UC - 1
                        ffn_half(half, i * FFN_CHUNKS + (c0 + n), i * 2 + (2 * FFN_STEPS * layer + half + 1))
                    if not (last and n + LEAD >= FFN_CHUNKS):
                        split_in_step(c0 + n + LEAD, i)

            load_ln_exp()
            for b in range(3):
                turned_hi(0, b)
                split(b)

            for u, kind in enumerate(UNITS0):
                for k in range(UC):
                    c = u * UC + k
                    if k == 0 and 7 <= u <= 14:
                        hgrn(u - 7, 8)
                    if k == 0 and 1 <= u <= N_IN0:
                        act.wait_ge(chunk_used, c)
                        read_acc(UNITS0[u - 1], u - 1).then_inc(acc_act, 1)
                    if u == 0:
                        split(c + LEAD)
                        if k + 3 < UC:
                            turned_hi(0, k + 3)
                        if k == 1:
                            act.dma_start(w1, w1_src[0]).then_inc(w1_loaded, 16)
                        if k == 6:
                            act.wait_ge(small_loaded, 48)
                            nc.scalar.activation(gwh[:], gw, ACT.Copy).then_inc(s_gwh, 1)
                        if k == 7:
                            act.wait_ge(s_lb, 1)
                            nc.scalar.activation(lbt[:], lbt[:], ACT.Exp).then_inc(s_lbe, 1)
                        if k == 6:
                            act.wait_ge(s_lam_ps, 1)
                            nc.scalar.activation(lam[:, 2:4], misc_ps[:, 0:2], ACT.Exp, scale=float(HD)).then_inc(s_lam_e, 1)
                    if u in (1, 3) and k == 3:
                        i = u // 2
                        act.wait_ge(s_hid_ps, i + 1)
                        nc.scalar.activation(hid[:], misc_ps[:, 0:2 * NCMP], ACT.Exp, scale=-1.0).then_inc(s_hid_e, 1)
                        if i == 0:
                            act.dma_start(w1, w1_src[1]).then_inc(w1_loaded, 16)
                    if u == 2 and k == 4:
                        act.wait_ge(s_gate_ps, 1)
                        nc.scalar.activation(gateT, misc_ps[0:NGATE, 0:T], ACT.Copy).then_inc(s_gate_c, 1)
                    if u == 2 and k == 5:
                        act.wait_ge(s_gate_T, 1)
                        nc.scalar.activation(gates[:], misc_ps[:, 0:NT * NGATE].rearrange("p (t n) -> p t n", t=NT),
                                             ACT.Exp, scale=-1.0).then_inc(s_gate_e, 1)
                    if u in (4, 5) and k == 3:
                        g = u - 4
                        act.wait_ge(s_cz, g + 1)
                        nc.scalar.activation(pc[g][:], pc[g][:], ACT.Exp, scale=SCALE).then_inc(s_ce, 1)
                    if nsa_head(u) is not None:
                        nsa(nsa_head(u), k)
                    if hgrn_head(u) is not None:
                        hgrn(hgrn_head(u), k)
                    if u:
                        split(c + LEAD)

            def feed_forward(layer, c0, e):
                layer_norm(2 * layer)
                for b in range(3):
                    turned_hi(e, b)
                for n in range(FFN_CHUNKS):
                    if n in (UC, 2 * UC):
                        half = n // UC - 1
                        ffn_half(half, c0 + n, 2 * FFN_STEPS * layer + half + 1)
                    split(c0 + n + LEAD)
                    if n + 3 < UC:
                        turned_hi(e, n + 3)
                    if n == 5:
                        load_silu()
                with act.Fori(1, FFN_STEPS - layer) as i:
                    ffn_step(layer, c0, i)
                if layer == 1:
                    ffn_step(layer, c0, FFN_STEPS - 1, last=True)
                load_ln_exp()
                layer_norm(2 * layer + 1)

            feed_forward(0, FFN0, 1)

            for b in range(3):
                turned_hi(2, b)
            for u, kind in enumerate(UNITS1):
                for k in range(UC):
                    c = L1 + u * UC + k
                    if k == 0 and 1 <= u <= len(UNITS1) - NB:
                        act.wait_ge(chunk_used, c)
                        read_acc(UNITS1[u - 1], u - 1).then_inc(acc_act, 1)
                    if u == 0:
                        split(c + LEAD)
                    if u == 0 and k + 3 < UC:
                        turned_hi(2, k + 3)
                    if u in WORK1:
                        what, i = WORK1[u]
                        (moba if what == "moba" else diff)(i, k)
                    if u:
                        split(c + LEAD)
            feed_forward(1, FFN1, 3)

        @block.vector
        def _(dve):
            steps = [0]

            def step(ins):
                steps[0] += 1
                ins.then_inc(dve_step, 1)
                dve.wait_ge(dve_step, steps[0])

            def split(c):
                dve.wait_ge(hi_done, c + 1)
                s = c % SPLIT_RING
                nc.vector.tensor_tensor(wl[s][:], raw[c % RAW_RING][:], wh[s][:].bitcast(F32), ALU.subtract).then_inc(lo_done, 1)

            def split_in_step(c, i):
                dve.wait_ge(hi_done, i * FFN_CHUNKS + (c + 1))
                s = c % SPLIT_RING
                nc.vector.tensor_tensor(wl[s][:], raw[c % RAW_RING][:], wh[s][:].bitcast(F32), ALU.subtract).then_inc(lo_done, 1)

            def turned_full(e, b):
                ps = pair(bank[2 + b % 6])
                dve.wait_ge(x_turned, UC * e + b + 1)
                if e == 0:
                    nc.vector.tensor_copy(xfull[b % 3], ps).then_inc(x_full, 1)
                    return
                for k in range(CK):
                    at = (e - 1) * KT + CK * b + k
                    ins = nc.vector.tensor_scalar(xfull[b % 3][:, k, :], ps[:, k, :], cols1[:, at:at + 1],
                                                  cols1[:, 64 + at:65 + at], ALU.mult, ALU.add)
                ins.then_inc(x_full, 1)

            def turned_lo(e, b):
                s = slice(CK * b, CK * b + CK)
                dve.wait_ge(x_hi, UC * e + b + 1)
                nc.vector.tensor_tensor(xl[:, s, :], xfull[b % 3], xh[:, s, :].bitcast(F32), ALU.subtract).then_inc(x_lo, 1)

            def turned_start(e):
                turned_full(e, 0)
                turned_full(e, 1)
                turned_lo(e, 0)
                turned_full(e, 2)
                turned_lo(e, 1)

            def turned_slot(e, k):
                if k + 3 < UC:
                    turned_full(e, k + 3)
                if k + 2 < UC:
                    turned_lo(e, k + 2)

            def add_block(cb, A, B, sem_done, count):
                cols = slice(cb * CW, (cb + 1) * CW)
                nc.vector.tensor_tensor(res[:, 0, cols], A[:], res[:, 0, cols], ALU.add)
                nc.vector.tensor_tensor(res[:, 1, cols], B[:], res[:, 1, cols], ALU.add).then_inc(sem_done, 1)
                dve.wait_ge(sem_done, count)
                for t in range(NT):
                    nc.vector.bn_stats(stats[:, t, cb, :], res[:, t, cols])

            def block_done(o, k):
                return {(1, OUT0_END): 0, (2, 0): 1, (3, 0): 2}.get((o, k))

            def out_block(layer, cb, n_in, used, residual):
                dve.wait_ge(chunk_used, used)
                if cb == 0:
                    dve.wait_ge(res_ready, residual)
                add_block(cb, *acc_banks(n_in + cb), acc_dve, acc_dve_count(layer, n_in + cb))

            def layer_norm(n):
                step(nc.vector.engine_nop())
                for t in range(NT):
                    ins = nc.vector.bn_aggr(mv[:, t, :], stats[:, t].rearrange("p b s -> p (b s)"))
                ins.then_inc(var_ready, 1)
                dve.wait_ge(rstd_ready, n + 1)
                nc.vector.tensor_scalar(shift[:], mv[:, 1, 0:1], rstd[:, 1:2], -1.0, ALU.mult, ALU.mult).then_inc(shift_ready, 1)
                for q in range(NB):
                    part = res[:, 0, q * CW:(q + 1) * CW]
                    nc.vector.tensor_scalar(part, part, mv[:, 0, 0:1], rstd[:, 0:1], ALU.subtract, ALU.mult).then_inc(x_normed, 1)

            def soft_max(m):
                dve.wait_ge(s_scores, m + 1)
                nc.vector.tensor_reduce(mx[:, 0:1], scores_ps[:, 0:P], AX.X, ALU.max)
                step(nc.vector.tensor_reduce(mx[:, 1:2], scores_ps[:, P:3 * P], AX.X, ALU.max))
                nc.vector.tensor_scalar(negmx[:], mx[:], -SCALE, None, ALU.mult).then_inc(s_negmx, 1)

            def soft_norm(m, n, gate=None):
                dve.wait_ge(s_exp, m + 1)
                f = fac[:, m % 2, :]
                step(nc.vector.reciprocal(f, rowsum[:, m % 2, :]))
                if gate is not None:
                    step(nc.vector.tensor_tensor(f, f, gates[:, :, gate], ALU.mult))
                p = prob[m % 2]
                nc.vector.tensor_scalar(p[:, 0:P], p[:, 0:P], f[:, 0:1], None, ALU.mult)
                nc.vector.tensor_scalar(p[:, P:3 * P], p[:, P:3 * P], f[:, 1:2], None, ALU.mult).then_inc(s_prob, 1)

            def plain_lo(kt, count):
                dve.wait_ge(s_oh, count)
                nc.vector.tensor_tensor(ol[:, kt, :], o_ps[:, 0:T], oh[:, kt, :].bitcast(F32), ALU.subtract).then_inc(s_ol, 1)

            def norm_lo(r, kt, w):
                dve.wait_ge(s_foh, r + 1)
                nc.vector.tensor_tensor(ol[:, kt:kt + w, :], of[:, 0:w, :], oh[:, kt:kt + w, :].bitcast(F32),
                                        ALU.subtract).then_inc(s_fol, 1)

            def read_acc(kind, u):
                A, B = acc_banks(u)
                if kind == "cmp":
                    return nc.vector.tensor_copy(cT[:, 2:4, :], pair(B))
                if kind in ("values", "mv0", "mv1", "dv0", "dv1"):
                    return nc.vector.tensor_copy(vnat[:, 1, :], B[:])
                if kind == "keys" or kind[1] == "p":
                    return nc.vector.tensor_copy(kT[:, 2:4, :], pair(B))
                i = int(kind[1])
                return nc.vector.tensor_copy(qT[:, HPG * i + 2:HPG * i + 4, :], pair(B))

            def make_blocks(i):
                for g in range(2):
                    z = cT[:, 2 * i + g, :].rearrange("p (n s) -> p s n", s=CMP_STRIDE)
                    for part in range(CMP_LEN // CMP_STRIDE):
                        at = C_POS + CMP_LEN * i + part * CMP_STRIDE
                        ins = nc.vector.tensor_tensor(
                            blk[:, part * CMP_STRIDE:(part + 1) * CMP_STRIDE, g, :], z[:, :, part:part + NCMP],
                            cols2[:, at:at + CMP_STRIDE].unsqueeze(2).to_broadcast([P, CMP_STRIDE, NCMP]), ALU.add)
                ins.then_inc(s_blk, 1)

            def hidden(i):
                dve.wait_ge(s_hid_e, i + 1)
                step(nc.vector.tensor_scalar(hid[:], hid[:], 1.0, None, ALU.add))
                step(nc.vector.reciprocal(hid[:], hid[:]))
                nc.vector.tensor_tensor(hid[:], misc_ps[:, 0:2 * NCMP], hid[:], ALU.mult).then_inc(s_hid, 1)

            def compressed(g, k):
                shape = [P, NT * HPG, NCMP]
                z = pc[g][:]
                if k == 1:
                    dve.wait_ge(s_cs, g + 1)
                    ps = misc_ps[:, 0:NT * HPG * NCMP].rearrange("p (a n) -> p a n", n=NCMP)
                    step(nc.vector.tensor_tensor(z, ps, cmask[:], ALU.mult))
                    step(nc.vector.tensor_tensor(z, z, cneg[:], ALU.add))
                    step(nc.vector.tensor_reduce(cmx[:], z, AX.X, ALU.max))
                    nc.vector.tensor_tensor(z, z, cmx[:].unsqueeze(2).to_broadcast(shape), ALU.subtract).then_inc(s_cz, 1)
                if k == 4:
                    dve.wait_ge(s_ce, g + 1)
                    step(nc.vector.tensor_reduce(csum[:], z, AX.X, ALU.add))
                    step(nc.vector.reciprocal(csum[:], csum[:]))
                    for t in range(NT):
                        gate = gates[:, t, :].rearrange("p (h c) -> p h c", c=3)[:, HPG * g:HPG * (g + 1), 0]
                        part = csum[:, t * HPG:(t + 1) * HPG]
                        ins = nc.vector.tensor_tensor(part, part, gate, ALU.mult)
                    step(ins)
                    step(nc.vector.tensor_tensor(z, z, cmask[:], ALU.mult))
                    nc.vector.tensor_tensor(z, z, csum[:].unsqueeze(2).to_broadcast(shape), ALU.mult).then_inc(s_pc, 1)

            def nsa(h, k):
                if k == 1:
                    soft_max(2 * h)
                if k == 2:
                    soft_norm(2 * h, 2 * h, 3 * h + 1)
                if k == 3:
                    soft_max(2 * h + 1)
                if k == 4:
                    soft_norm(2 * h + 1, 2 * h + 1, 3 * h + 2)
                if k == 6:
                    plain_lo(8 + h, h + 1)

            def hgrn(h, k):
                u = 5 + h
                A, B = acc_banks(u)
                if k == 1:
                    dve.wait_ge(s_hsig, h + 1)
                    nc.vector.tensor_tensor(hx[:, 0, :], A[:, 0:T], hx[:, 0, :], ALU.mult)
                    nc.vector.tensor_scalar(hx[:, 1, :], hx[:, 1, :], lbc[:, 1, h:h + 1], lbc[:, 0, h:h + 1],
                                            ALU.mult, ALU.add).then_inc(s_hf, 1)
                    dve.wait_ge(s_hf, 2 * h + 1)
                    nc.vector.tensor_scalar(hk[:], hx[:, 1, :], -1.0, 1.0, ALU.mult, ALU.add)
                    nc.vector.tensor_tensor(hg[:], B[:, T:2 * T], hx[:, 2, :], ALU.mult).then_inc(acc_dve, 1)
                if k == 2:
                    dve.wait_ge(s_hlog, h + 1)
                    nc.vector.tensor_tensor_scan(hs[:], reset[:], hb[:], 0.0, ALU.mult, ALU.add).then_inc(s_hsum, 1)
                if k == 3:
                    dve.wait_ge(s_hvT, h + 1)
                    nc.vector.tensor_copy(hv[:], misc_ps[:, 0:T].rearrange("p (t v) -> p t v", t=NT)).then_inc(s_hv, 1)
                if k == 4:
                    dve.wait_ge(s_hexp, h + 1)
                    step(nc.vector.tensor_copy(hdec[:], he[:].rearrange("p (n c) -> p n c", c=HCHUNK)[:, :, HCHUNK - 1]))
                    nc.vector.tensor_tensor(he[:], he[:], hx[:, 0, :], ALU.mult).then_inc(s_hf, 1)
                    nc.vector.tensor_tensor(hn[:, 0, :], hn[:, 0, :], hk[:], ALU.mult)
                    nc.vector.tensor_tensor(hn[:, 1, :], hn[:, 1, :], hk[:], ALU.mult).then_inc(s_hqk, 1)
                if k == 5:
                    dve.wait_ge(s_hA, h + 1)
                    nc.vector.copy_predicated(hatt[:], omask[:], misc_ps[:, 0:T].rearrange("p (t c) -> p t c", t=NT)).then_inc(s_hatt, 1)
                if k == 6:
                    dve.wait_ge(s_hu, h + 1)
                    step(nc.vector.tensor_copy(hstate[:, 0, :], misc_ps[:, 0:HD]))
                    for n in range(1, NHC - 1):
                        ins = nc.vector.scalar_tensor_tensor(hstate[:, n, :], hstate[:, n - 1, :], hdec[:, n:n + 1],
                                                             misc_ps[:, n * HD:(n + 1) * HD], ALU.mult, ALU.add)
                        if n < NHC - 2:
                            step(ins)
                    ins.then_inc(s_hstate, 1)
                if k == 7:
                    dve.wait_ge(s_of, h + 1)
                    nc.vector.tensor_tensor(sq[:, 0, :], of[:, 0, :], of[:, 0, :], ALU.mult).then_inc(s_sq, 1)
                if k == 8:
                    dve.wait_ge(s_root, h + 1)
                    step(nc.vector.scalar_tensor_tensor(of[:, 0, :], of[:, 0, :], cols2[:, C_NORM:C_NORM + 1],
                                                        rootb[:, 1, :], ALU.mult, ALU.mult))
                    nc.vector.tensor_tensor(of[:, 0, :], of[:, 0, :], hg[:], ALU.mult).then_inc(s_fin, 1)
                    norm_lo(h, h, 1)

            def moba(i, k):
                m, head = N_MAPS0 + 2 * i, N_PLAIN0 + 2 * i
                if k == 1:
                    soft_max(m)
                if k == 2:
                    soft_max(m + 1)
                    soft_norm(m, m)
                if k == 3:
                    soft_norm(m + 1, m + 1)
                if k == 4:
                    plain_lo(2 * i, head + 1)
                if k == 6:
                    plain_lo(2 * i + 1, head + 2)

            def diff(d, k):
                m, n, r = 24 + 2 * d, 24 + d, N_NORM0 + d
                if k == 1:
                    soft_max(m)
                if k == 2:
                    soft_max(m + 1)
                if k == 3:
                    dve.wait_ge(s_exp, m + 2)
                    step(nc.vector.reciprocal(fac[:], rowsum[:]))
                    step(nc.vector.tensor_scalar(fac[:, 1, :], fac[:, 1, :], lam[:, 5:6], None, ALU.mult))
                    for q, cols in enumerate((slice(0, P), slice(P, 3 * P))):
                        ins = nc.vector.tensor_scalar(prob[0][:, cols], prob[0][:, cols], fac[:, 0, q:q + 1], None, ALU.mult)
                    step(ins)
                    for q, cols in enumerate((slice(0, P), slice(P, 3 * P))):
                        ins = nc.vector.scalar_tensor_tensor(prob[0][:, cols], prob[1][:, cols], fac[:, 1, q:q + 1],
                                                             prob[0][:, cols], ALU.mult, ALU.add)
                    ins.then_inc(s_prob, 1)
                if k == 5:
                    dve.wait_ge(s_of, r + 1)
                    nc.vector.tensor_tensor(sq[:], of[:], of[:], ALU.mult).then_inc(s_sq, 1)
                if k == 6:
                    dve.wait_ge(s_root, r + 1)
                    for t in range(2):
                        ins = nc.vector.scalar_tensor_tensor(of[:, t, :], of[:, t, :], lam[:, 6 + t:7 + t],
                                                             rootb[:, 1, :], ALU.mult, ALU.mult)
                    ins.then_inc(s_fin, 1)
                    norm_lo(r, 8 + 2 * d, 2)

            def ffn_half(half, count):
                dve.wait_ge(ffn_silu, count)
                nc.vector.tensor_tensor(ff, pair(bank[2 * half + 1]), fs, ALU.mult).then_inc(ffn_h, 1)
                dve.wait_ge(ffn_hh, count)
                s = slice(2 * half, 2 * half + 2)
                nc.vector.tensor_tensor(fl[:, s, :], ff, fh[:, s, :].bitcast(F32), ALU.subtract).then_inc(ffn_hl, 1)

            def ffn_block(cb, used, count):
                dve.wait_ge(chunk_used, used)
                a, b = FFN_BANKS[cb]
                add_block(cb, bank[a], bank[b], ffn_acc, count)

            block_end = {2 * UC + 2: 0, 2 * UC + 3: 1, 2 * UC + 5: 2, 2 * UC + 7: 3}

            def ffn_step(layer, c0, i, last=False):
                for n in range(FFN_CHUNKS + 1):
                    if n in (UC, 2 * UC):
                        half = n // UC - 1
                        ffn_half(half, i * 2 + (2 * FFN_STEPS * layer + half + 1))
                    if n < FFN_CHUNKS and not (last and n + LEAD >= FFN_CHUNKS):
                        split_in_step(c0 + n + LEAD, i)
                    if n - 1 in block_end:
                        cb = block_end[n - 1]
                        ffn_block(cb, i * FFN_CHUNKS + (c0 + n), i * NB + (FFN_ACC * layer + NB + cb + 1))

            turned_full(0, 0)
            turned_full(0, 1)
            turned_lo(0, 0)
            split(0)
            turned_full(0, 2)
            turned_lo(0, 1)
            split(1)
            split(2)

            for u, kind in enumerate(UNITS0):
                for k in range(UC):
                    c = u * UC + k
                    if block_done(u - N_IN0, k) is not None:
                        out_block(0, block_done(u - N_IN0, k), N_IN0, c, 1)
                    if k == 0 and 1 <= u <= N_IN0 and UNITS0[u - 1][0] != "h":
                        dve.wait_ge(chunk_used, c)
                        read_acc(UNITS0[u - 1], u - 1).then_inc(acc_dve, 1)
                    if k == 0 and 7 <= u <= 14:
                        hgrn(u - 7, 8)
                    if u == 0:
                        split(c + LEAD)
                        turned_slot(0, k)
                        if k == 4:
                            dve.wait_ge(rows_turned, 1)
                            nc.vector.tensor_copy(cols1[:], row_cols(0)).then_inc(cols_ready, 1)
                            nc.vector.tensor_copy(cols2[:], row_cols(1)).then_inc(cols_ready, 1)
                            dve.wait_ge(cols_ready, 2)
                            for i in range(2):
                                a = C_LAM + 2 * i
                                ins = nc.vector.tensor_tensor(lam[:, i:i + 1], cols2[:, a:a + 1], cols2[:, a + 1:a + 2], ALU.mult)
                            ins.then_inc(s_lam, 1)
                            nc.vector.tensor_scalar(lam[:, 6:8], cols2[:, C_SUB:C_SUB + 2], 1.0 - LAM_INIT, None, ALU.mult)
                        if k == 5:
                            lb3 = [cols2[:, C_LB + 8 * i:C_LB + 8 * (i + 1)] for i in range(3)]
                            step(nc.vector.tensor_tensor(lbm[:, 0, :], lb3[0], lb3[1], ALU.max))
                            step(nc.vector.tensor_tensor(lbm[:, 1, :], lbm[:, 0, :], lb3[2], ALU.max))
                            for i in range(3):
                                ins = nc.vector.tensor_tensor(lbt[:, i, :], lb3[i], lbm[:, 1, :], ALU.subtract)
                            ins.then_inc(s_lb, 1)
                        if k == 6:
                            dve.wait_ge(s_gwh, 1)
                            nc.vector.tensor_tensor(gwl[:], gw, gwh[:].bitcast(F32), ALU.subtract).then_inc(s_gwl, 1)
                        if k == 7:
                            dve.wait_ge(s_lbe, 1)
                            step(nc.vector.tensor_tensor(lbm[:, 0, :], lbt[:, 0, :], lbt[:, 1, :], ALU.add))
                            step(nc.vector.tensor_tensor(lbm[:, 1, :], lbm[:, 0, :], lbt[:, 2, :], ALU.add))
                            step(nc.vector.reciprocal(lbm[:, 0, :], lbm[:, 1, :]))
                            step(nc.vector.tensor_tensor(lbc[:, 0, :], lbt[:, 0, :], lbm[:, 0, :], ALU.mult))
                            step(nc.vector.tensor_scalar(lbc[:, 1, :], lbc[:, 0, :], -1.0, 1.0, ALU.mult, ALU.add))
                            dve.wait_ge(s_lam_e, 1)
                            step(nc.vector.tensor_tensor(lam[:, 4:5], lam[:, 3:4], lam[:, 2:3], ALU.subtract))
                            step(nc.vector.tensor_scalar(lam[:, 5:6], lam[:, 4:5], -LAM_INIT, None, ALU.add))
                    if u == 1 and k == 0:
                        dve.wait_ge(acc_act, 1)
                        step(nc.vector.engine_nop())
                        make_blocks(0)
                    if u in (1, 3) and k == 3:
                        hidden(u // 2)
                    if u == 1 and k == 5:
                        dve.wait_ge(s_cmp_ps, 1)
                        nc.vector.tensor_copy(kcmp[:], misc_ps[:, 64:64 + 2 * NCMP]).then_inc(s_cmp, 1)
                    if u == 2 and k == 0:
                        dve.wait_ge(s_hid_ps, 1)
                        make_blocks(1)
                    if u == 3 and k == 5:
                        dve.wait_ge(s_cmp_ps, 2)
                        nc.vector.tensor_copy(vcmp[:], misc_ps[0:NCMP, T:2 * T].rearrange("p (g c) -> p g c", g=2)).then_inc(s_cmp, 1)
                    if u == 2 and k == 6:
                        dve.wait_ge(s_gate_e, 1)
                        step(nc.vector.tensor_scalar(gates[:], gates[:], 1.0, None, ALU.add))
                        nc.vector.reciprocal(gates[:], gates[:]).then_inc(s_gates, 1)
                        dve.wait_ge(s_gates, 1)
                    if u in (4, 5):
                        compressed(u - 4, k)
                    if nsa_head(u) is not None:
                        nsa(nsa_head(u), k)
                    if hgrn_head(u) is not None:
                        hgrn(hgrn_head(u), k)
                    if u:
                        split(c + LEAD)

            def feed_forward(layer, c0, e, units, u_last):
                dve.wait_ge(chunk_used, c0)
                add_block(NB - 1, *acc_banks(u_last), acc_dve, acc_dve_count(layer, u_last))
                layer_norm(2 * layer)
                turned_start(e)
                for _ in range(NB):
                    dve.sem_inc(ffn_acc, 1)
                for n in range(FFN_CHUNKS + 1):
                    if n in (UC, 2 * UC):
                        half = n // UC - 1
                        ffn_half(half, 2 * FFN_STEPS * layer + half + 1)
                    if n < FFN_CHUNKS:
                        split(c0 + n + LEAD)
                    if n < UC:
                        turned_slot(e, n)
                    if n - 1 in block_end:
                        cb = block_end[n - 1]
                        if cb == 0:
                            dve.wait_ge(res_ready, e + 1)
                        ffn_block(cb, c0 + n, FFN_ACC * layer + NB + cb + 1)
                with dve.Fori(1, FFN_STEPS - layer) as i:
                    ffn_step(layer, c0, i)
                if layer == 1:
                    ffn_step(layer, c0, FFN_STEPS - 1, last=True)
                layer_norm(2 * layer + 1)

            feed_forward(0, FFN0, 1, UNITS0, len(UNITS0) - 1)

            turned_start(2)
            for u, kind in enumerate(UNITS1):
                for k in range(UC):
                    c = L1 + u * UC + k
                    n_in = len(UNITS1) - NB
                    if block_done(u - n_in, k) is not None:
                        out_block(1, block_done(u - n_in, k), n_in, c, 3)
                    if k == 0 and 1 <= u <= n_in:
                        dve.wait_ge(chunk_used, c)
                        read_acc(UNITS1[u - 1], u - 1).then_inc(acc_dve, 1)
                    if u == 0:
                        split(c + LEAD)
                        turned_slot(2, k)
                    if u in WORK1:
                        what, i = WORK1[u]
                        (moba if what == "moba" else diff)(i, k)
                    if u:
                        split(c + LEAD)
            feed_forward(1, FFN1, 3, UNITS1, len(UNITS1) - 1)

            dve.wait_ge(lnw_loaded, 32 * 4)
            dve.wait_ge(x_normed, 4 * NB)
            dve.wait_ge(x_normed_act, 4 * NB)
            for q in range(NB):
                cols = slice(q * CW, (q + 1) * CW)
                for t in range(NT):
                    ins = nc.vector.tensor_tensor(res[:, t, cols], res[:, t, cols], wb[:, 0, cols], ALU.mult)
                step(ins)
                for t in range(NT):
                    ins = nc.vector.tensor_tensor(res[:, t, cols], res[:, t, cols], wb[:, 1, cols], ALU.add)
                ins.then_inc(out_ready, 1)

        @block.tensor
        def _(pe):
            def turned(e):
                for b in range(UC):
                    ps = bank[2 + b % 6]
                    if e and b % 2 == 0:
                        pe.wait_ge(x_normed, NB * (e - 1) + b // 2 + 1)
                        pe.wait_ge(x_normed_act, NB * (e - 1) + b // 2 + 1)
                    if e == 0 and b % 2 == 0:
                        pe.wait_ge(x_loaded[b // 2], 16)
                    if b >= 6:
                        pe.wait_ge(x_full, UC * e + b - 5)
                    for k in range(CK):
                        at = (CK * b + k) * P
                        for t in range(NT):
                            ins = nc.tensor.transpose(ps[:, (k * NT + t) * P:(k * NT + t + 1) * P], res[:, t, at:at + P], ident[:])
                    ins.then_inc(x_turned, 1)

            def parts(s):
                return ((wh[s], False), (wh[s], True), (wl[s], False))

            def by_weights(c, j, n, acc, start):
                s = c % SPLIT_RING
                for k in range(CK):
                    for w, low in parts(s):
                        x_part = xl if low else xh
                        ins = nc.tensor.matmul(acc, w[:, k, n * P:(n + 1) * P], x_part[:, CK * j + k, :],
                                               start=start and k == 0 and w is wh[s] and not low,
                                               stop=j == UC - 1 and k == CK - 1 and w is wl[s], skip_group_check=True)
                return ins

            def by_tokens(c, kts, t, acc, cols, start, stop, xs):
                s = c % SPLIT_RING
                x_hi_part, x_lo_part = xs
                for k, kt in enumerate(kts):
                    for w, low in parts(s):
                        x_part = x_lo_part if low else x_hi_part
                        ins = nc.tensor.matmul(acc, x_part[:, kt, t * P:(t + 1) * P], w[:, k, cols],
                                               start=start and k == 0 and w is wh[s] and not low,
                                               stop=stop and k == CK - 1 and w is wl[s], skip_group_check=True)
                return ins

            def project(layer, u, kind, c, j):
                A, B = acc_banks(u)
                pe.wait_ge(lo_done, c + 1)
                if j == 0 and u >= 2:
                    pe.wait_ge(acc_dve, acc_dve_count(layer, u - 2))
                    if (UNITS0, UNITS1)[layer][u - 2] != "out":
                        pe.wait_ge(acc_act, acc_act_count(layer, u - 2))
                if u == 0:
                    pe.wait_ge(x_lo, UC * 2 * layer + j + 1)
                kts = (CK * j, CK * j + 1)
                last = j == UC - 1
                if kind == "out":
                    kt = out_ktile(layer, j)
                    for t, acc in enumerate((A, B)):
                        ins = by_tokens(c, (kt, kt + 1), t, acc[:], slice(0, CW), j == 0, last, (oh, ol))
                elif kind in ("values", "mv0", "mv1", "dv0", "dv1"):
                    for t, acc in enumerate((A, B)):
                        ins = by_tokens(c, kts, t, acc[:], slice(0, CW), j == 0, last, (xh, xl))
                else:
                    for n in range(4):
                        acc = (A, B)[n // 2]
                        ins = by_weights(c, j, n, acc[:, (n % 2) * T:(n % 2 + 1) * T], j == 0 and n % 2 == 0)
                ins.then_inc(chunk_used, 1)

            def mm(ps, w, x_part, start=True, stop=True):
                return nc.tensor.matmul(ps, w, x_part, start=start, stop=stop, skip_group_check=True)

            def map_scores(m, q, k):
                if m:
                    pe.wait_ge(s_exp, m)
                mm(scores_ps[:, 0:P], q[:, 0:P], k[:, 0:P], True, False)
                mm(scores_ps[:, 0:P], identb[:], negmask[:], False, True)
                mm(scores_ps[:, P:3 * P], q[:, P:2 * P], k, False, False)
                mm(scores_ps[:, 2 * P:3 * P], identb[:], negmask[:], False, True).then_inc(s_scores, 1)

            def map_turn(n, p):
                pe.wait_ge(s_prob, n + 1)
                if n:
                    pe.wait_ge(s_pTc, n)
                for i in range(3):
                    ins = nc.tensor.transpose(pT_ps[:, i * P:(i + 1) * P], p[:, i * P:(i + 1) * P], ident[:])
                ins.then_inc(s_pT, 1)

            def map_values(n, v_cols, acc, start, stop):
                pe.wait_ge(s_pTc, n + 1)
                mm(acc, vnat[:, 0, v_cols], pT[:, 0:T], start, False)
                return mm(acc[:, P:T], vnat[:, 1, v_cols], pT[:, T:T + P], False, stop)

            def nsa(h, k):
                g = h // HPG
                if k == 0:
                    if h == 0 or h == HPG:
                        pe.wait_ge(acc_act, acc_act_count(0, 3 + g))
                        pe.wait_ge(acc_dve, acc_dve_count(0, 3 + g))
                    map_scores(2 * h, qT[:, h, :], kT[:, g, :])
                if k == 1:
                    pe.wait_ge(s_pc, g + 1)
                    if h:
                        pe.wait_ge(s_pTc, 2 * h)
                    for t in range(NT):
                        ins = nc.tensor.transpose(pT_ps[0:NCMP, t * P:(t + 1) * P], pc[g][:, t * HPG + h % HPG, :], ident[:])
                    ins.then_inc(s_pcT, 1)
                if k == 2:
                    map_scores(2 * h + 1, qT[:, h, :], kT[:, 2 + g, :])
                    pe.wait_ge(s_pcTc, h + 1)
                    map_turn(2 * h, prob[0])
                if k == 3:
                    if h:
                        pe.wait_ge(s_ol, h)
                    mm(o_ps[:, 0:T], vcmp[:, g, :], pcT[:], True, False)
                    map_values(2 * h, slice(g * HD, (g + 1) * HD), o_ps[:, 0:T], False, False).then_inc(s_pv, 1)
                if k == 4:
                    map_turn(2 * h + 1, prob[1])
                if k == 5:
                    map_values(2 * h + 1, slice((2 + g) * HD, (3 + g) * HD), o_ps[:, 0:T], False, True).then_inc(s_pv, 1)

            def hgrn(h, k):
                if k == 2:
                    if h:
                        pe.wait_ge(s_root, h)
                    else:
                        pe.wait_ge(s_cz, 2)
                    pe.wait_ge(acc_act, acc_act_count(0, 5 + h))
                    for t in range(NT):
                        ins = nc.tensor.transpose(misc_ps[:, t * P:(t + 1) * P], hv[:, t, :], ident[:])
                    ins.then_inc(s_hvT, 1)
                if k == 4:
                    pe.wait_ge(s_hv, h + 1)
                    pe.wait_ge(s_hqk, h + 1)
                    for t in range(NT):
                        s = slice(t * P, (t + 1) * P)
                        mm(misc_ps[:, s], hn[:, 0, s], he[:, s], t == 0, True)
                    for t in range(NT):
                        ins = nc.tensor.transpose(misc_ps[:, T + t * P:T + (t + 1) * P], hn[:, 1, t * P:(t + 1) * P], ident[:])
                    ins.then_inc(s_hA, 1)
                if k == 5:
                    pe.wait_ge(s_hk2, h + 1)
                    for n in (0, 2, 1):
                        if n == 1:
                            pe.wait_ge(s_hu_even, h + 1)
                        t, r = n // 2, slice((n % 2) * HCHUNK, (n % 2 + 1) * HCHUNK)
                        ins = mm(misc_ps[:, n * HD:(n + 1) * HD], hk2[r, t, :], hv[r, t, :], n == 0, True)
                        if n == 2:
                            ins.then_inc(s_hu_even, 1)
                    ins.then_inc(s_hu, 1)
                if k == 6:
                    pe.wait_ge(s_hatt, h + 1)
                    pe.wait_ge(s_hstate, h + 1)
                    for t in range(NT):
                        s = slice(t * P, (t + 1) * P)
                        mm(misc_ps[:, s], hv[:, t, :], hatt[:, t, :], t == 0, False)
                    for n in range(1, NHC):
                        s = slice(n * HCHUNK, (n + 1) * HCHUNK)
                        ins = mm(misc_ps[:, s], hstate[:, n - 1, :], he[:, s], False, True)
                    ins.then_inc(s_ho, 1)
                if k == 7:
                    pe.wait_ge(s_sq, h + 1)
                    mm(misc_ps[:, 0:T], means[:], sq[:, 0, :]).then_inc(s_ms, 1)

            def moba(i, k):
                m, head = N_MAPS0 + 2 * i, N_PLAIN0 + 2 * i
                if k in (0, 1):
                    if k == 0:
                        pe.wait_ge(acc_act, acc_act_count(1, moba_unit(i)))
                        pe.wait_ge(acc_dve, acc_dve_count(1, moba_unit(i)))
                    map_scores(m + k, kT[:, k, :], kT[:, 2 + k, :])
                if k in (2, 4):
                    map_turn(m + (k - 2) // 2, prob[(k - 2) // 2])
                if k in (3, 5):
                    j = (k - 3) // 2
                    pe.wait_ge(s_ol, head + j)
                    v = (2 * i + j) % 4 * HD
                    map_values(m + j, slice(v, v + HD), o_ps[:, 0:T], True, True).then_inc(s_pv, 1)

            def moba_unit(i):
                return 1 + i + i // 2

            def diff(d, k):
                m, n, r = 24 + 2 * d, 24 + d, N_NORM0 + d
                if k in (0, 1):
                    if k == 0:
                        pe.wait_ge(acc_act, acc_act_count(1, 6 + moba_unit(d)))
                        pe.wait_ge(acc_dve, acc_dve_count(1, 6 + moba_unit(d)))
                    map_scores(m + k, kT[:, k, :], kT[:, 2 + k, :])
                if k == 3:
                    map_turn(n, prob[0])
                if k == 4:
                    pe.wait_ge(s_ol, 16)
                    pe.wait_ge(s_of, r)
                    for t in range(2):
                        v = (d % 2) * 2 * HD + t * HD
                        ins = map_values(n, slice(v, v + HD), o_ps[:, t * T:(t + 1) * T], t == 0, True)
                    ins.then_inc(s_pv, 1)
                if k == 5:
                    pe.wait_ge(s_root, r)
                    pe.wait_ge(s_sq, r + 1)
                    mm(misc_ps[:, 0:T], means[:], sq[:, 0, :], True, False)
                    mm(misc_ps[:, 0:T], means[:], sq[:, 1, :], False, True).then_inc(s_ms, 1)

            def out_ready_for(layer, j):
                if layer == 0:
                    if j == 0:
                        pe.wait_ge(s_ol, N_PLAIN0)
                    if j >= 4:
                        pe.wait_ge(s_fol, 2 * (j - 4) + 2)
                else:
                    if j == 0:
                        pe.wait_ge(s_ol, 16)
                    if j >= 4:
                        pe.wait_ge(s_fol, N_NORM0 + (j - 4) + 1)

            def ffn_step(layer, c0, i, first=False):
                acc0 = FFN_ACC * layer
                h0 = 2 * FFN_STEPS * layer
                for n in range(FFN_CHUNKS):
                    c = c0 + n
                    pe.wait_ge(lo_done, i * FFN_CHUNKS + (c + 1))
                    if n < 2 * UC:
                        half, j = n // UC, n % UC
                        if first and half == 0:
                            pe.wait_ge(x_lo, UC * (2 * layer + 1) + j + 1)
                        if j == 0:
                            pe.wait_ge(ffn_acc, i * NB + (acc0 + 3 + half))
                        for m in range(4):
                            acc = bank[2 * half + m // 2]
                            ins = by_weights(c, j, m, acc[:, (m % 2) * T:(m % 2 + 1) * T], j == 0 and m % 2 == 0)
                    else:
                        cb, kk = OUT_ORDER[n - 2 * UC]
                        if kk == 0:
                            if cb < 2:
                                pe.wait_ge(ffn_acc, i * NB + (acc0 + 1 + cb))
                            else:
                                pe.wait_ge(ffn_h, i * 2 + (h0 + cb - 1))
                        if cb == 0:
                            pe.wait_ge(ffn_hl, i * 2 + (h0 + kk + 1))
                        for t in range(NT):
                            ins = by_tokens(c, (CK * kk, CK * kk + 1), t, bank[FFN_BANKS[cb][t]][:], slice(0, CW),
                                            kk == 0, kk == 1, (fh, fl))
                    ins.then_inc(chunk_used, 1)

            pe.wait_ge(const_ready, 1)
            turned(0)
            for u, kind in enumerate(UNITS0):
                for k in range(UC):
                    if kind == "out":
                        cb, j = OUT_STREAM[(u - N_IN0) * UC + k]
                        if cb == 0:
                            out_ready_for(0, j)
                        project(0, N_IN0 + cb, kind, u * UC + k, j)
                    else:
                        project(0, u, kind, u * UC + k, k)
                    if u == 0 and k == 3:
                        pe.wait_ge(const_ready, 10)
                        pe.wait_ge(rows_loaded, 16 * 11)
                        nc.tensor.transpose(row_cols(0), rows1[:], ident[:])
                        nc.tensor.transpose(row_cols(1), rows2[:], ident[:]).then_inc(rows_turned, 1)
                    if u == 0 and k == 5:
                        pe.wait_ge(s_lam, 1)
                        mm(misc_ps[:, 0:2], means[:], lam[:, 0:2]).then_inc(s_lam_ps, 1)
                    if u in (1, 3) and k == 2:
                        i = u // 2
                        pe.wait_ge(s_blk, i + 1)
                        pe.wait_ge(w1_loaded, 16 * (i + 1))
                        if i == 0:
                            pe.wait_ge(s_lam_e, 1)
                        else:
                            pe.wait_ge(s_gates, 1)
                        for l in range(CMP_LEN):
                            ins = mm(misc_ps[:, 0:2 * NCMP], w1[:, l, :], blk[:, l].rearrange("p g n -> p (g n)"),
                                     l == 0, l == CMP_LEN - 1)
                        ins.then_inc(s_hid_ps, 1)
                    if u == 1 and k == 4:
                        pe.wait_ge(s_hid, 1)
                        mm(misc_ps[:, 64:64 + 2 * NCMP], w2[:, 0, :], hid[:]).then_inc(s_cmp_ps, 1)
                    if u == 3 and k == 4:
                        pe.wait_ge(s_hid, 2)
                        for g in range(2):
                            ins = mm(misc_ps[0:NCMP, T + g * HD:T + (g + 1) * HD], hid[:, g * NCMP:(g + 1) * NCMP],
                                     w2[:, 1, :], g == 0, True)
                        ins.then_inc(s_cmp_ps, 1)
                    if u == 2 and k == 3:
                        pe.wait_ge(s_gwl, 1)
                        pe.wait_ge(s_cmp, 1)
                        for kt in range(KT):
                            for w, x_part in ((gwh, xh), (gwh, xl), (gwl, xh)):
                                ins = mm(misc_ps[0:NGATE, 0:T], w[:, kt, :], x_part[:, kt, :],
                                         kt == 0 and w is gwh and x_part is xh, kt == KT - 1 and w is gwl)
                        ins.then_inc(s_gate_ps, 1)
                    if u == 2 and k == 4:
                        pe.wait_ge(s_gate_c, 1)
                        for t in range(NT):
                            ins = nc.tensor.transpose(misc_ps[:, t * NGATE:(t + 1) * NGATE], gateT[:, t * P:(t + 1) * P],
                                                      ident[0:NGATE, 0:NGATE])
                        ins.then_inc(s_gate_T, 1)
                    if u in (4, 5) and k == 0:
                        g = u - 4
                        pe.wait_ge(acc_act, acc_act_count(0, 3 + g))
                        pe.wait_ge(acc_dve, acc_dve_count(0, 3 + g))
                        pe.wait_ge(s_cmp, 2)
                        if g:
                            pe.wait_ge(s_cz, 1)
                        for t in range(NT):
                            for h in range(HPG):
                                at = (t * HPG + h) * NCMP
                                ins = mm(misc_ps[:, at:at + NCMP], qT[:, HPG * g + h, t * P:(t + 1) * P],
                                         kcmp[:, g * NCMP:(g + 1) * NCMP], t == 0 and h == 0, True)
                        ins.then_inc(s_cs, 1)
                    if nsa_head(u) is not None:
                        nsa(nsa_head(u), k)
                    if hgrn_head(u) is not None:
                        hgrn(hgrn_head(u), k)

            turned(1)
            ffn_step(0, FFN0, 0, first=True)
            with pe.Fori(1, FFN_STEPS) as i:
                ffn_step(0, FFN0, i)

            turned(2)
            for u, kind in enumerate(UNITS1):
                for k in range(UC):
                    if kind == "out":
                        cb, j = OUT_STREAM[(u - len(UNITS1) + NB) * UC + k]
                        if cb == 0:
                            out_ready_for(1, j)
                        project(1, len(UNITS1) - NB + cb, kind, L1 + u * UC + k, j)
                    else:
                        project(1, u, kind, L1 + u * UC + k, k)
                    if u in WORK1:
                        what, i = WORK1[u]
                        (moba if what == "moba" else diff)(i, k)
            turned(3)
            ffn_step(1, FFN1, 0, first=True)
            with pe.Fori(1, FFN_STEPS) as i:
                ffn_step(1, FFN1, i)


_INS = ['x', 'ln_w', 'ln_b', 'ffn_w_in', 'ffn_w_out', 'ab_w_in', 'ab_w_out', 'hgrn_lower_bounds', 'hgrn_norm_w',
        'nsa_cmp_pos_k', 'nsa_cmp_k_w1', 'nsa_cmp_k_w2', 'nsa_cmp_pos_v', 'nsa_cmp_v_w1', 'nsa_cmp_v_w2',
        'cd_w_in', 'cd_w_out', 'diff_lambda_q1', 'diff_lambda_k1', 'diff_lambda_q2', 'diff_lambda_k2', 'diff_subln_w']
_OUTS = [((1, T, D), 'float32')]


def kernel(**inputs):
    import numpy as _np
    import concourse.bacc as _bacc
    from concourse import mybir as _mybir
    from concourse.bass_utils import run_bass_kernel_spmd as _run

    nc = _bacc.Bacc("TRN2", target_bir_lowering=False, num_devices=1)
    arrays, args = {}, []
    for name in _INS:
        a = _np.ascontiguousarray(inputs[name])
        arrays[f"in_{name}_dram"] = a
        args.append(nc.dram_tensor(f"in_{name}_dram", a.shape, _mybir.dt.from_np(a.dtype), kind="ExternalInput").ap())
    for i, (shape, dtype) in enumerate(_OUTS):
        dt = _mybir.dt.from_np(_np.dtype(dtype))
        args.append(nc.dram_tensor(f"out_{i}_dram", shape, dt, kind="ExternalOutput").ap())
    build(nc, *args)
    r = _run(nc, [arrays], core_ids=[0])
    return r.results[0]["out_0_dram"]
```
